# Optimizing a Trainium2 kernel written in Bass

```python
import math
import jax
import jax.numpy as jnp
from jax import lax
import numpy as np

D_MODEL = 1024
BATCH = 1
SEQ = 512
DEPTH = 2

A_HEADS = 6
A_KDIM = 128
A_VDIM = 64
A_CHUNK = 64
B_HEADS = 6
B_HDIM = 64
B_BLOCK = 128
C_GROUPS = ((128, 1), (512, 4), (2048, 16))
C_HEADS_PER_GROUP = 4
C_HEADS = C_HEADS_PER_GROUP * len(C_GROUPS)
C_HDIM = 64
C_BLOCK = 128
D_FF = 2816
N_BRANCH = 3
N_NORMS = 6
EPS = 1e-6
NEG_BIG = -1e30
TINY = 1e-30

A_QK = A_HEADS * A_KDIM
A_V = A_HEADS * A_VDIM
B_W = B_HEADS * B_HDIM
C_W = C_HEADS * C_HDIM
C_OUT = C_HEADS_PER_GROUP * C_HDIM
IN_COLS = 2 * A_QK + 2 * A_V + 3 * B_W + 3 * C_W + N_BRANCH * D_MODEL

kernel_name = 'hybrid_hgrn2_stickbreak_dilated_macaron'

def rms_norm(x, g):
    xf = x.astype(jnp.float32)
    y = xf * lax.rsqrt(jnp.mean(xf * xf, axis=-1, keepdims=True) + EPS)
    return (y * g.astype(jnp.float32)).astype(x.dtype)

def swiglu_ffn(h, w_in, w_out):
    a, b = jnp.split(h @ w_in, 2, axis=-1)
    return (jax.nn.silu(a) * b) @ w_out

def alibi_slopes(n):
    def pow2_slopes(m):
        start = 2.0 ** (-8.0 / m)
        return [start ** (i + 1) for i in range(m)]
    if math.log2(n).is_integer():
        s = pow2_slopes(n)
    else:
        c = 2 ** int(math.floor(math.log2(n)))
        s = pow2_slopes(c) + pow2_slopes(2 * c)[0::2][: n - c]
    return sorted(s, reverse=True)

def hgrn2_mixer(q, f_raw, i, g, lb, norm_g):
    f32 = jnp.float32
    bsz, seq, nh, kd = q.shape
    vd = i.shape[-1]
    lb = lb.astype(f32)
    f_raw = f_raw.astype(f32)
    qf = jax.nn.silu(q.astype(f32))
    f = lb + (1.0 - lb) * jax.nn.sigmoid(f_raw)
    log_f = jnp.log(jnp.maximum(f, TINY))
    kf = (1.0 - lb) * jax.nn.sigmoid(-f_raw)
    vf = i.astype(f32)
    n = seq // A_CHUNK

    def to_chunks(t):
        return t.reshape(bsz, n, A_CHUNK, nh, t.shape[-1]).transpose(1, 0, 3, 2, 4)

    causal = jnp.tril(jnp.ones((A_CHUNK, A_CHUNK), dtype=bool))

    def step(state, xs):
        qc, kc, vc, lfc = xs
        b = jnp.cumsum(lfc, axis=2)
        o_inter = jnp.einsum('bhtk,bhkv->bhtv', qc * jnp.exp(b), state)
        diff = b[:, :, :, None, :] - b[:, :, None, :, :]
        decay = jnp.exp(jnp.where(causal[:, :, None], diff, NEG_BIG))
        scores = jnp.einsum('bhtk,bhsk,bhtsk->bhts', qc, kc, decay)
        o_intra = jnp.einsum('bhts,bhsv->bhtv', scores, vc)
        b_end = b[:, :, -1:, :]
        new_state = (jnp.exp(b_end[:, :, 0, :])[..., None] * state
                     + jnp.einsum('bhsk,bhsv->bhkv', kc * jnp.exp(b_end - b), vc))
        return new_state, o_inter + o_intra

    state0 = jnp.zeros((bsz, nh, kd, vd), f32)
    _, o = lax.scan(step, state0, (to_chunks(qf), to_chunks(kf), to_chunks(vf), to_chunks(log_f)))
    o = o.transpose(1, 0, 3, 2, 4).reshape(bsz, seq, nh, vd)
    o = rms_norm(o, norm_g) * jax.nn.silu(g.astype(f32))
    return o.reshape(bsz, seq, nh * vd)

def stick_breaking_mixer(q, k, v):
    f32 = jnp.float32
    bsz, seq, nh, d = q.shape
    qh, kh, vh = (t.astype(f32).transpose(0, 2, 1, 3) for t in (q, k, v))
    nb = seq // B_BLOCK
    q_blocks = qh.reshape(bsz, nh, nb, B_BLOCK, d).transpose(2, 0, 1, 3, 4)
    starts = jnp.arange(nb) * B_BLOCK
    key_pos = jnp.arange(seq)
    scale = d ** -0.5

    def block(args):
        qb, t0 = args
        z = jnp.einsum('bhtd,bhsd->bhts', qb, kh) * scale
        causal = key_pos[None, :] < (t0 + jnp.arange(B_BLOCK))[:, None]
        log_1m = jnp.where(causal, jax.nn.log_sigmoid(-z), 0.0)
        suffix = lax.cumsum(log_1m, axis=3, reverse=True) - log_1m
        a = jnp.where(causal, jnp.exp(jnp.where(causal, jax.nn.log_sigmoid(z) + suffix, NEG_BIG)), 0.0)
        return jnp.einsum('bhts,bhsd->bhtd', a, vh)

    o = lax.map(block, (q_blocks, starts))
    return o.transpose(1, 0, 3, 2, 4).reshape(bsz, seq, nh * d)

def dilated_group_attention(q, k, v, window, dilation, slopes):
    f32 = jnp.float32
    bsz, seq, nh, d = q.shape
    sub_len = seq // dilation
    nb = -(-sub_len // C_BLOCK)
    lp = nb * C_BLOCK
    pad = lp - sub_len

    def strided(t):
        return t.astype(f32).reshape(bsz, sub_len, dilation, nh, d).transpose(0, 2, 3, 1, 4)

    qs = jnp.pad(strided(q), ((0, 0), (0, 0), (0, 0), (0, pad), (0, 0)))
    ks = jnp.pad(strided(k), ((0, 0), (0, 0), (0, 0), (C_BLOCK, pad), (0, 0)))
    vs = jnp.pad(strided(v), ((0, 0), (0, 0), (0, 0), (C_BLOCK, pad), (0, 0)))
    blk = (bsz, dilation, nh, nb, C_BLOCK, d)
    qb = qs.reshape(blk)
    kb = jnp.concatenate([ks[:, :, :, :lp].reshape(blk), ks[:, :, :, C_BLOCK:].reshape(blk)], axis=4)
    vb = jnp.concatenate([vs[:, :, :, :lp].reshape(blk), vs[:, :, :, C_BLOCK:].reshape(blk)], axis=4)
    s = jnp.einsum('brhnid,brhnjd->brhnij', qb, kb) * d ** -0.5
    qi = jnp.arange(C_BLOCK)[:, None]
    kj = jnp.arange(2 * C_BLOCK)[None, :]
    delta = qi + C_BLOCK - kj
    key_idx = (jnp.arange(nb) * C_BLOCK)[:, None, None] + kj[None] - C_BLOCK
    valid = (delta >= 0) & (delta <= window // dilation) & (key_idx >= 0)
    bias = -slopes[:, None, None, None] * (delta * dilation).astype(f32)
    s = jnp.where(valid, s + bias, NEG_BIG)
    m = jnp.max(s, axis=-1, keepdims=True)
    p = jnp.exp(s - m)
    den = jnp.sum(p, axis=-1, keepdims=True)
    o = jnp.einsum('brhnij,brhnjd->brhnid', p, vb) / den
    lse = (m + jnp.log(den))[..., 0]
    o = o.reshape(bsz, dilation, nh, lp, d)[:, :, :, :sub_len].transpose(0, 3, 1, 2, 4).reshape(bsz, seq, nh, d)
    lse = lse.reshape(bsz, dilation, nh, lp)[:, :, :, :sub_len].transpose(0, 3, 1, 2).reshape(bsz, seq, nh)
    return o, lse

def dilated_mixer(q, k, v):
    bsz, seq = q.shape[:2]
    slopes = jnp.asarray(alibi_slopes(C_HEADS), jnp.float32)
    outs, lses = [], []
    for gi, (w, r) in enumerate(C_GROUPS):
        sl = slice(gi * C_HEADS_PER_GROUP, (gi + 1) * C_HEADS_PER_GROUP)
        o, lse = dilated_group_attention(q[:, :, sl], k[:, :, sl], v[:, :, sl], w, r, slopes[sl])
        outs.append(o)
        lses.append(lse)
    wts = jax.nn.softmax(jnp.stack(lses, axis=2), axis=2)
    o = jnp.sum(wts[..., None] * jnp.stack(outs, axis=2), axis=2)
    return o.reshape(bsz, seq, C_OUT)

def token_mixing(h, w_in, lb, a_norm_g, w_br_a, w_br_b, w_br_c, w_out):
    bsz, seq, _ = h.shape
    widths = [A_QK, A_QK, A_V, A_V, B_W, B_W, B_W, C_W, C_W, C_W]
    idx = [int(v) for v in np.cumsum(widths)]
    aq, af, ai, ag, bq, bk, bv, cq, ck, cv, gate_logits = jnp.split(h @ w_in, idx, axis=-1)

    def heads(t, n):
        return t.reshape(bsz, seq, n, -1)

    ya = hgrn2_mixer(heads(aq, A_HEADS), heads(af, A_HEADS), heads(ai, A_HEADS), heads(ag, A_HEADS),
                     lb.reshape(A_HEADS, A_KDIM), a_norm_g)
    yb = stick_breaking_mixer(heads(bq, B_HEADS), heads(bk, B_HEADS), heads(bv, B_HEADS))
    yc = dilated_mixer(heads(cq, C_HEADS), heads(ck, C_HEADS), heads(cv, C_HEADS))
    gates = jax.nn.sigmoid(gate_logits.reshape(bsz, seq, N_BRANCH, D_MODEL).astype(jnp.float32)).astype(h.dtype)
    merged = (gates[:, :, 0] * (ya.astype(h.dtype) @ w_br_a)
              + gates[:, :, 1] * (yb.astype(h.dtype) @ w_br_b)
              + gates[:, :, 2] * (yc.astype(h.dtype) @ w_br_c))
    return merged @ w_out

def modulated_sublayer(x, fn, g_pre, g_post, m, res_w):
    shift, scale, gate = m[:, 0][:, None], m[:, 1][:, None], m[:, 2][:, None]
    h = rms_norm(x, g_pre) * (1.0 + scale) + shift
    return x + res_w * gate * rms_norm(fn(h), g_post)

def setup_inputs(seed: int = 0) -> dict:
    key = jax.random.key(seed)
    ks = jax.random.split(key, 18)
    nrm = jax.random.normal
    f32 = jnp.float32
    return {
        'x': nrm(ks[0], (BATCH, SEQ, D_MODEL), f32),
        'c': nrm(ks[1], (BATCH, D_MODEL), f32),
        'w_ada': nrm(ks[2], (DEPTH, D_MODEL, 9 * D_MODEL), f32) * (0.5 * D_MODEL ** -0.5),
        'b_ada': nrm(ks[3], (DEPTH, 9 * D_MODEL), f32) * 0.01,
        'norm_g': 1.0 + 0.05 * nrm(ks[4], (DEPTH, N_NORMS, D_MODEL), f32),
        'ffn1_w_in': nrm(ks[5], (DEPTH, D_MODEL, 2 * D_FF), f32) * D_MODEL ** -0.5,
        'ffn1_w_out': nrm(ks[6], (DEPTH, D_FF, D_MODEL), f32) * D_FF ** -0.5,
        'w_in': nrm(ks[7], (DEPTH, D_MODEL, IN_COLS), f32) * D_MODEL ** -0.5,
        'hgrn_lb_logits': nrm(ks[8], (DEPTH, A_QK), f32),
        'hgrn_norm_g': 1.0 + 0.05 * nrm(ks[9], (DEPTH, A_VDIM), f32),
        'w_branch_a': nrm(ks[10], (DEPTH, A_V, D_MODEL), f32) * A_V ** -0.5,
        'w_branch_b': nrm(ks[11], (DEPTH, B_W, D_MODEL), f32) * B_W ** -0.5,
        'w_branch_c': nrm(ks[12], (DEPTH, C_OUT, D_MODEL), f32) * C_OUT ** -0.5,
        'w_out': nrm(ks[13], (DEPTH, D_MODEL, D_MODEL), f32) * D_MODEL ** -0.5,
        'ffn2_w_in': nrm(ks[14], (DEPTH, D_MODEL, 2 * D_FF), f32) * D_MODEL ** -0.5,
        'ffn2_w_out': nrm(ks[15], (DEPTH, D_FF, D_MODEL), f32) * D_FF ** -0.5,
    }

def reference(x, c, w_ada, b_ada, norm_g, ffn1_w_in, ffn1_w_out, w_in, hgrn_lb_logits, hgrn_norm_g,
              w_branch_a, w_branch_b, w_branch_c, w_out, ffn2_w_in, ffn2_w_out):
    bsz = x.shape[0]
    lb_p = jax.nn.softmax(hgrn_lb_logits.astype(jnp.float32), axis=0)
    lb_all = jnp.cumsum(lb_p, axis=0) - lb_p[0:1]
    c_act = jax.nn.silu(c)
    for l in range(DEPTH):
        mod = (c_act @ w_ada[l] + b_ada[l]).reshape(bsz, 3, 3, D_MODEL)
        x = modulated_sublayer(x, lambda h: swiglu_ffn(h, ffn1_w_in[l], ffn1_w_out[l]),
                               norm_g[l, 0], norm_g[l, 1], mod[:, 0], 0.5)
        x = modulated_sublayer(x, lambda h: token_mixing(h, w_in[l], lb_all[l], hgrn_norm_g[l], w_branch_a[l],
                                                         w_branch_b[l], w_branch_c[l], w_out[l]),
                               norm_g[l, 2], norm_g[l, 3], mod[:, 1], 1.0)
        x = modulated_sublayer(x, lambda h: swiglu_ffn(h, ffn2_w_in[l], ffn2_w_out[l]),
                               norm_g[l, 4], norm_g[l, 5], mod[:, 2], 0.5)
    return x


_drawn_inputs = setup_inputs


def setup_inputs(seed=0):
    import zlib

    import numpy as np

    out = dict(_drawn_inputs(seed))
    spreads = {}
    factors = {'b_ada': 2.873, 'hgrn_lb_logits': 4.549, 'hgrn_norm_g': 4.134}
    for name, (base, spread) in spreads.items():
        noise = np.random.default_rng([zlib.crc32(name.encode()), seed]).standard_normal(out[name].shape)
        drawn = base * np.exp(spread * noise) if base else spread * noise
        out[name] = jnp.asarray(drawn.astype(out[name].dtype))
    for name, factor in factors.items():
        out[name] = (out[name] * factor).astype(out[name].dtype)
    return out
```

```python
import math
from contextlib import ExitStack

import numpy as np

import concourse.bass as bass
from concourse import mybir

F32 = mybir.dt.float32
F32R = mybir.dt.float32r
U8 = mybir.dt.uint8
ALU = mybir.AluOpType
ACT = mybir.ActivationFunctionType
AX = mybir.AxisListType

P = 128
D = 1024
SEQ = 512
DEPTH = 2
KT = D // P
TT = SEQ // P
DFF = 2816
FT = DFF // P
EPS = 1e-6
NEG_BIG = -1e30
TINY = 1e-30

A_HEADS, A_V = 6, 64
B_HEADS, HD = 6, 64
C_HEADS, C_SLOTS = 12, 4
A_LEVELS = 7
QSCALE = HD ** -0.5
LN_LIFT = 2.0 ** 40

FI, FO = FT, FT // 2
COL_AQ, COL_AF, COL_AI, COL_AG = 0, 768, 1536, 1920
COL_BQ, COL_BK, COL_BV = 2304, 2688, 3072
COL_CQ, COL_CK, COL_CV = 3456, 4224, 4992
COL_GATE = 5760
_TOKENS = [("av", COL_AI, 256), ("av", COL_AI + 256, 128), ("ag", COL_AG, 256), ("ag", COL_AG + 256, 128),
           ("bv", COL_BV, 256), ("bv", COL_BV + 256, 128)]
MIX = ([x for h in range(A_HEADS) for x in (("a", COL_AQ + P * h, COL_AF + P * h), _TOKENS[h])]
       + [("b", COL_BQ + P * p, COL_BK + P * p) for p in range(3)]
       + [("cv", COL_CV + 256 * i, 256) for i in range(3)]
       + [("c", COL_CQ + P * p, COL_CK + P * p) for p in range(6)]
       + [("gate", COL_GATE + 256 * i, 256) for i in range(12)])
ITEM_B, ITEM_C, ITEM_GATE = 12, 18, 24
PAIR_KINDS = ("a", "b", "c")
TOKEN_KINDS = ("av", "ag", "bv", "cv")
NM = len(MIX)
G_FFN1, G_FO1 = 0, FI
G_MIX = G_FO1 + FO
G_BR = G_MIX + NM
G_WO = G_BR + 4
G_FFN2 = G_WO + 4
G_FO2 = G_FFN2 + FI
NG = G_FO2 + FO
assert NG % 2 == 0


def group_columns(g):
    if G_MIX <= g < G_BR and MIX[g - G_MIX][0] not in PAIR_KINDS:
        return KT * MIX[g - G_MIX][2]
    return 2048


TILE0 = [0]
for kind, _, _ in MIX:
    TILE0.append(TILE0[-1] + (TT if kind in TOKEN_KINDS else 2))
NTILES = TILE0[-1]
assert NTILES % 2 == 0


ROW_LASTS = (G_MIX - 1, G_FFN2 - 1, NG - 1)


def used_count(g):
    return sum(x not in ROW_LASTS for x in range(g + 1))


def loads_of(g):
    return 3 if G_BR <= g < G_WO else 2


def loads_until(g):
    return sum(loads_of(x) for x in range(g % 2, g + 1, 2))


LOADS = [loads_until(NG - 2), loads_until(NG - 1)]

ADA_ALL = 9 * D // SEQ
ADA_CHUNKS = (FI // 2, ADA_ALL - FI // 2)
ADA_FIRST = ADA_CHUNKS[1]
ADA_BEFORE = (0, ADA_CHUNKS[0])
assert 4 * ADA_FIRST >= 3 * KT and DEPTH == 2

CONST = {}
_at = 0
for _name, _n in (("ident", P), ("ones", P), ("ntri", P), ("nones", P), ("strict", P), ("negm", P),
                  ("reset", SEQ), ("del0", TT * 2 * P), ("del1", P), ("del2", P)):
    CONST[_name] = (_at, _n)
    _at += _n
NCONST = _at


def alibi_slopes(n):
    def pow2(m):
        start = 2.0 ** (-8.0 / m)
        return [start ** (i + 1) for i in range(m)]
    c = 2 ** int(math.floor(math.log2(n)))
    s = pow2(n) if c == n else pow2(c) + pow2(2 * c)[0::2][: n - c]
    return [float(np.float32(x)) for x in sorted(s, reverse=True)]


def constants():
    t = np.zeros((P, NCONST), np.float32)
    i, j = np.arange(P)[:, None], np.arange(P)[None, :]

    def put(name, a):
        at, n = CONST[name]
        t[:, at:at + n] = np.broadcast_to(a, (P, n))

    put("ident", (i == j) * 1.0)
    put("ones", 1.0)
    put("ntri", (i >= j) * -1.0)
    put("nones", -1.0)
    put("strict", (i < j) * 1.0)
    put("negm", np.where(i < j, 0.0, NEG_BIG))
    put("reset", (np.arange(SEQ)[None, :] % P != 0) * 1.0)
    tile, key = np.arange(TT)[:, None], np.arange(2 * P)[None, :]
    delta = i[:, :, None] + P - key[None]
    valid = (delta >= 0) & (delta <= P) & (P * (tile[None] - 1) + key[None] >= 0)
    put("del0", np.where(valid, -delta, NEG_BIG).reshape(P, -1))
    put("del1", np.where(i >= j, -4.0 * (i - j), NEG_BIG))
    put("del2", np.where((i >= j) & ((i - j) % 4 == 0), -4.0 * (i - j), NEG_BIG))
    return t


def level_masks():
    m = np.zeros((P, A_LEVELS, P // 2), np.float32)
    for lev in range(A_LEVELS):
        w = P >> lev
        for t in range(P // 2):
            b = t // (w // 2)
            m[b * w:b * w + w // 2, lev, t] = 1
    return m.reshape(P, -1)


def build(nc, t, out):
    ctx = ExitStack()
    with ctx:
        body(nc, ctx, t, out)


def body(nc, ctx, t, out):
    slopes = alibi_slopes(C_HEADS)
    base = (nc.sbuf_base + 31) // 32 * 32
    at = [base]

    def sb(name, shape, dtype=F32, offset=None):
        size = int(np.prod(shape[1:])) * (1 if dtype == U8 else 4)
        if offset is None:
            offset, at[0] = at[0], at[0] + (size + 31) // 32 * 32
        assert offset + size <= nc.sbuf_usable_end, (name, offset + size, nc.sbuf_usable_end)
        return nc.alloc_sbuf_tensor_at(name, shape, dtype, offset=offset)

    X = sb("X", [P, KT, SEQ])
    HH = sb("HH", [P, KT, SEQ], F32R)
    HL = sb("HL", [P, KT, SEQ], F32R)
    RAW = [sb(f"RAW{i}", [P, 2048]) for i in range(2)]
    WH = [sb(f"WH{i}", [P, 2048], F32R) for i in range(2)]
    WL = [sb(f"WL{i}", [P, 2048], F32R) for i in range(2)]
    CT = sb("CT", [P, NCONST])
    LM = sb("LM", [P, A_LEVELS, P // 2], U8)
    CC = sb("CC", [P, KT])
    COLS = sb("COLS", [P, DEPTH, 120])
    MOD = sb("MOD", [P, 72])
    PRE = sb("PRE", [P, 3, KT])
    POST = sb("POST", [P, 3, KT])
    LB = sb("LB", [P, DEPTH, A_HEADS])
    LBW = sb("LBW", [P, 4, A_HEADS])
    LBC = sb("LBC", [P, A_HEADS])
    OML = sb("OML", [P, A_HEADS])
    EPSC = sb("EPSC", [P, 1])
    NGR = sb("NGR", [P, A_V])
    phase = at[0]

    def const(name):
        a, n = CONST[name]
        return CT[:, a:a + n]

    ident, ones = const("ident"), const("ones")

    GH = sb("GH", [P, FT, SEQ], F32R, phase)
    GL = sb("GL", [P, FT, SEQ], F32R, phase + FT * 2048)
    at[0] = phase + 2 * FT * 2048
    SB = [sb(f"SB{i}", [P, SEQ]) for i in range(2)]
    AW = [sb(f"AW{i}", [P, SEQ]) for i in range(2)]
    AACC = [sb("AACC0", [P, SEQ])]
    AWB = [sb(f"AWB{i}", [P, KT, SEQ], F32, phase + 16384 * i) for i in range(2)]
    AACC.append(sb("AACC1", [P, SEQ], F32, phase + 69632))
    Y = sb("Y", [P, KT, SEQ], F32, phase)
    NSQ = [sb(f"NSQ{i}", [P, 2, SEQ], F32, phase + 16384 + 4096 * i) for i in range(2)]
    NSS = [sb(f"NSS{i}", [P, SEQ], F32, phase + 24576 + 2048 * i) for i in range(2)]
    NLN = sb("NLN", [P, SEQ], F32, phase + 28672)
    NR = sb("NR", [P, SEQ], F32, phase + 30720)
    U = sb("U", [P, KT, SEQ], F32, phase + 32768)
    XIN = sb("XIN", [P, TT, D], F32, phase + 49152)
    ROWS = sb("ROWS", [P, P], F32, phase + 65536)
    LMF = sb("LMF", [P, A_LEVELS * P // 2], F32, phase + 66560)
    ROWL = [sb(f"ROWL{i}", [P, P], F32, phase + 68608 + 512 * i) for i in range(DEPTH)]

    OA = sb("OA", [P, TT, A_HEADS * A_V], F32, phase)
    OB = sb("OB", [P, TT, B_HEADS * HD], F32, phase + 6144)
    OF = sb("OF", [P, TT, C_SLOTS * HD], F32, phase + 12288)
    r1 = phase + 16384
    AQ = [sb(f"AQ{i}", [P, SEQ], F32, r1 + 2048 * i) for i in range(2)]
    AB = [sb(f"AB{i}", [P, SEQ], F32, r1 + 4096 + 2048 * i) for i in range(2)]
    AK = [sb(f"AK{i}", [P, SEQ], F32, r1 + 8192 + 2048 * i) for i in range(2)]
    AV = sb("AV", [P, TT, A_HEADS * A_V], F32, r1 + 12288)
    GN = sb("GN", [P, TT, A_HEADS * A_V], F32, r1 + 18432)
    QF = sb("QF", [P, 2, SEQ], F32, r1 + 24576)
    W1 = sb("W1", [P, 2, SEQ], F32, r1 + 28672)
    W2 = sb("W2", [P, 2, SEQ], F32, r1 + 32768)
    MK = sb("MK", [P, SEQ], U8, r1 + 36864)
    AD = [sb(f"AD{i}", [P, SEQ], F32, r1 + 37376 + 2048 * i) for i in range(2)]
    AE = [sb(f"AE{i}", [P, SEQ], F32, r1 + 41472 + 2048 * i) for i in range(2)]
    KL = [sb(f"KL{i}", [P, SEQ], F32, r1 + 45568 + 2048 * i) for i in range(2)]
    QL = [sb(f"QL{i}", [P, TT, P // 2], F32, r1 + 49664 + 1024 * i) for i in range(2)]
    AS = [sb(f"AS{i}", [P, TT, P], F32, r1 + 51712 + 2048 * i) for i in range(2)]
    QB = [sb(f"QB{i}", [P, SEQ], F32, r1 + 55808 + 2048 * i) for i in range(2)]
    EB = sb("EB", [P, SEQ], F32, r1 + 59904)
    KD = sb("KD", [P, SEQ], F32, r1 + 61952)
    KDT = sb("KDT", [P, TT - 1, P], F32, r1 + 64000)
    ST = [sb(f"ST{i}", [P, TT - 1, A_V], F32, r1 + 65536 + 768 * i) for i in range(2)]
    ARS = sb("ARS", [P, 3, TT * A_HEADS], F32, r1 + 67072)
    ASQ = sb("ASQ", [P, TT, A_HEADS * A_V], F32, r1 + 55808)
    BQ = [sb(f"BQ{i}", [P, SEQ], F32, r1 + 67584 + 2048 * i) for i in range(2)]
    BK = [sb(f"BK{i}", [P, SEQ], F32, r1 + 71680 + 2048 * i) for i in range(2)]
    BV = sb("BV", [P, TT, B_HEADS * HD], F32, r1 + 75776)
    BZ = [sb(f"BZ{i}", [P, 1280], F32, r1 + 24576 + 5120 * i) for i in range(2)]
    BS = [sb(f"BS{i}", [P, 1280], F32, r1 + 34816 + 5120 * i) for i in range(2)]
    BA = [sb(f"BA{i}", [P, 1280], F32, r1 + 45056 + 5120 * i) for i in range(2)]
    CV = sb("CV", [P, TT, C_HEADS, HD + 1], F32, r1)
    CQ = [sb(f"CQ{i}", [P, SEQ], F32, r1 + 12480 + 2048 * i) for i in range(2)]
    CK = [sb(f"CK{i}", [P, SEQ], F32, r1 + 16576 + 2048 * i) for i in range(2)]
    CS = [sb(f"CS{i}", [P, SEQ], F32, r1 + 24576 + 2048 * i) for i in range(2)]
    CP = [sb(f"CP{i}", [P, SEQ], F32, r1 + 28672 + 2048 * i) for i in range(2)]
    CPT = [sb(f"CPT{i}", [P, SEQ], F32, r1 + 32768 + 2048 * i) for i in range(2)]
    OC = sb("OC", [P, TT, C_HEADS, HD + 2], F32, r1 + 55296)
    OCN = sb("OCN", [P, TT, 8, HD + 2], F32, r1 + 67968)
    CW = sb("CW", [P, 5, TT * C_SLOTS], F32, r1 + 24576)
    CX = [sb(f"CX{i}", [P, TT, C_SLOTS, HD + 1], F32, r1 + 24960 + 4160 * i) for i in range(2)]
    gate_at = ([20672 + 32] + [36864 + 2048 * i for i in range(9)] + [76416 + 2048 * i for i in range(4)]
               + [24576 + 2048 * i for i in range(6)] + [67968 + 2048 * i for i in range(4)])
    GT = [sb(f"GT{i}", [P, SEQ], F32, r1 + o) for i, o in enumerate(gate_at)]
    y_at = [2048 * i for i in range(10)] + [55296 + 2048 * i for i in range(6)]
    YH = [sb(f"YH{i}", [P, SEQ], F32R, r1 + y_at[i]) for i in range(KT)]
    YL = [sb(f"YL{i}", [P, SEQ], F32R, r1 + y_at[KT + i]) for i in range(KT)]
    MA = [sb(f"MA{i}", [P, 3, SEQ], F32, phase + 6144 * i) for i in range(2)]

    PS = ctx.enter_context(nc.psum_tensor("PS", [P, 8, 512], F32))

    of_a_layer = []

    def sig(name, per_layer=0):
        sem = ctx.enter_context(nc.semaphore(name))
        if per_layer:
            of_a_layer.append(sem)
        return sem

    const_in, c_rows_in, x_in = sig("const_in"), sig("c_rows_in"), sig("x_in")
    c_turned, c_out_of_psum, c_act, lb_exp = sig("c_turned"), sig("c_out_of_psum"), sig("c_act"), sig("lb_exp")
    lb_step, lb_part, eps_set, mask_set = sig("lb_step"), sig("lb_part"), sig("eps_set"), sig("mask_set")
    x_turned, x_out = sig("x_turned"), sig("x_out")
    rowl_in, cols_turned, cols_out = sig("rowl_in"), sig("cols_turned"), sig("cols_out")
    first_in, first_part, first_sum, first_out = (
        [sig(f"first_in{i}") for i in range(2)], sig("first_part"), sig("first_sum"), sig("first_out"))
    res_turned, res_out, stored = sig("res_turned"), sig("res_out"), sig("stored")

    loaded = [sig(f"loaded{i}", 16 * LOADS[i]) for i in range(2)]
    w_high, w_low, w_used = sig("w_high", NG), sig("w_low", NG), sig("w_used", used_count(NG - 1))
    part_high = sig("part_high", 3 * (NM - 2))
    ngr_in, lb_out = sig("ngr_in", 16), sig("lb_out", 1)
    ada_in = [sig(f"ada_in{j}", 16 * 18 * KT // 2) for j in range(2)]
    ada_part, ada_sum, ada_out, ada_cols = (
        sig("ada_part", 19 * KT), sig("ada_sum", 18), sig("ada_out", 18), sig("ada_cols", 8))
    n_sq, n_ss, n_mm, n_ln, n_r = sig("n_sq", 48), sig("n_ss", 24), sig("n_mm", 24), sig("n_ln", 6), sig("n_r", 6)
    y_done, y_copied, y_scaled, x_even, x_odd = (
        sig(n, c) for n, c in (("y_done", 24), ("y_copied", 24), ("y_scaled", 24), ("x_even", 12), ("x_odd", 12)))
    u_done, h_high, f_odd, h_low_even, h_low_odd = (
        sig("u_done", 24), sig("h_high", 24), sig("f_odd", 12), sig("h_low_even", 12), sig("h_low_odd", 12))
    a_done, silu_done, gated, g_high, g_low = (sig(n, 2 * FT) for n in ("a_done", "silu_done", "gated", "g_high", "g_low"))
    tile_done = sig("tile_done", NTILES - NM)
    tile_out = [sig(f"tile_out{i}", NTILES // 2) for i in range(2)]
    p_abs, p_e, p_ln, p_ls, p_t, p_sg, p_sn, p_q, p_k = (
        sig(n, A_HEADS) for n in ("p_abs", "p_e", "p_ln", "p_ls", "p_t", "p_sg", "p_sn", "p_q", "p_k"))
    p_f, p_lf, p_log, p_mask = sig("p_f", 3 * A_HEADS), sig("p_lf", 2 * A_HEADS), sig("p_log", 3 * A_HEADS), sig("p_mask", A_HEADS)
    NL = A_HEADS * A_LEVELS
    v_diff, v_decay, v_scaled, v_mm, v_out = (sig(n, NL) for n in ("v_diff", "v_decay", "v_scaled", "v_mm", "v_out"))
    i_diag, i_s0, i_diff, i_decay, i_kd, i_eb, i_qb, i_turn, i_kdt, i_u, i_o, i_oout = (
        sig(n, A_HEADS) for n in ("i_diag", "i_s0", "i_diff", "i_decay", "i_kd", "i_eb", "i_qb", "i_turn", "i_kdt",
                                  "i_u", "i_o", "i_oout"))
    i_st, kl_set = sig("i_st", 3 * A_HEADS), sig("kl_set", 2)
    gn_silu, an, an_ln, an_r = sig("gn_silu", 1), sig("an", 5), sig("an_ln", 1), sig("an_r", 1)
    b_z, b_abs, b_e, b_ln, b_sp, b_spm, b_arg, b_a, b_pv, b_out = (
        sig(n, B_HEADS) for n in ("b_z", "b_abs", "b_e", "b_ln", "b_sp", "b_spm", "b_arg", "b_a", "b_pv", "b_out"))
    units = [(h, i) for h in range(C_HEADS) for i in ((0, 2) if h < C_SLOTS else (0,))]
    NU = len(units)
    c_s, c_bias, c_max, c_sub, c_p, c_t, c_pt, c_pv, c_out = (
        sig(n, NU) for n in ("c_s", "c_bias", "c_max", "c_sub", "c_p", "c_t", "c_pt", "c_pv", "c_out"))
    c_ones, c_perm, cmb, cmb_e = sig("c_ones", 1), sig("c_perm", 16 * 16), sig("cmb", 10), sig("cmb_e", 1)
    cmb_x = sig("cmb_x", 1)
    yt_done, yt_high, yt_low = sig("yt_done", KT), sig("yt_high", KT), sig("yt_low", KT)
    g_sig = sig("g_sig", 24)
    br_done, br_mul, br_add, m_high, m_low, br_sum = (
        sig("br_done", KT // 2), sig("br_mul", KT), sig("br_add", KT), sig("m_high", KT), sig("m_low", KT), sig("br_sum", KT))

    def units_of(pair):
        return [n for n, (h, _) in enumerate(units) if h // 2 == pair]

    UNIT_AT = {}
    for pair in range(C_HEADS // 2):
        for q, n in enumerate(units_of(pair)):
            UNIT_AT[(ITEM_C + 1 + pair, q * 8 // len(units_of(pair)))] = n
    UNIT_AT[(ITEM_C + 7, 0)], UNIT_AT[(ITEM_C + 7, 3)] = NU, NU + 1
    ITEM_COMBINE, ITEM_TURN = 27, 28

    def used(g):
        return (y_done, KT * (ROW_LASTS.index(g) + 1)) if g in ROW_LASTS else (w_used, used_count(g))

    def projected(m, i):
        return used(G_MIX + m) if i == TILE0[m + 1] - TILE0[m] - 1 else (tile_done, TILE0[m] - m + i + 1)

    def taken(tile):
        return tile_out[tile % 2], tile // 2 + 1

    def z_at(i, h):
        return {0: (2 + 3 * (h % 2), 0), 1: (3 + 3 * (h % 2), 0), 3: (3 + 3 * (h % 2), 384), 2: (4 + 3 * (h % 2), 0)}[i]

    ZCOL = {0: 0, 1: 512, 3: 896, 2: 1024}

    def zw(i):
        return SEQ - P * i

    def level_view(ap, lev, half=None):
        w = P >> lev
        v = ap.rearrange("p (b w) -> p b w", w=w)
        return v if half is None else v[:, :, half * (w // 2):(half + 1) * (w // 2)]

    with nc.Block() as block:
        @block.sync
        def _(sp):
            sp.dma_start(CT[:, :], t["const_f"]).then_inc(const_in, 16)
            sp.dma_start(LMF[:, :], t["const_m"]).then_inc(const_in, 16)
            sp.dma_start(ROWS[0:8, :], t["c"].rearrange("o (k p) -> (o k) p", p=P)).then_inc(c_rows_in, 16)
            sp.dma_start(ROWS[8:20, :], t["hgrn_lb_logits"].rearrange("l (k p) -> (l k) p", p=P)).then_inc(c_rows_in, 16)
            w = t["w_ada"].rearrange("l (k p) c -> p l k c", p=P)
            for ch in range(ADA_FIRST):
                if ch >= 2:
                    sp.wait_ge(first_part, KT * (ch - 1))
                sp.dma_start(AWB[ch % 2][:, :, :], w[:, 0, :, ch * SEQ:(ch + 1) * SEQ]).then_inc(first_in[ch % 2], 16)
                if ch == 0:
                    for l in range(DEPTH):
                        sp.dma_start(ROWL[l][0:72, :], t["b_ada"][l].rearrange("(k p) -> k p", p=P)).then_inc(rowl_in, 16)
                        sp.dma_start(ROWL[l][72:120, :], t["norm_g"][l].rearrange("n (k p) -> (n k) p", p=P)).then_inc(rowl_in, 16)
                    sp.dma_start(XIN[:, :, :], t["x"].rearrange("o (t p) d -> p (o t) d", p=P)).then_inc(x_in, 16)

        @block.tensor
        def _(pe):
            pe.wait_ge(const_in, 32)
            pe.wait_ge(c_rows_in, 32)
            pe.transpose(PS[:, 0, 0:20], ROWS[0:20, :], ident[0:20, 0:20]).then_inc(c_turned, 1)
            pe.wait_ge(x_in, 16)
            for k in range(KT):
                if k >= 2:
                    pe.wait_ge(x_out, k - 1)
                for i in range(TT):
                    mm = pe.transpose(PS[:, 1 + k % 2, i * P:(i + 1) * P], XIN[:, i, k * P:(k + 1) * P], ident)
                mm.then_inc(x_turned, 1)
            pe.wait_ge(rowl_in, 32 * DEPTH)
            for l in range(DEPTH):
                pe.transpose(PS[:, 3, l * P:l * P + 120], ROWL[l][0:120, :], ident[0:120, 0:120]).then_inc(cols_turned, 1)
            for ch in range(ADA_FIRST):
                pe.wait_ge(first_part, KT * (ch + 1))
                for q in range(4):
                    mm = pe.matmul(PS[:, 4 + ch % 2, q:q + 1], AACC[ch % 2][:, q * P:(q + 1) * P], ones[:, 0:1],
                                   start=True, stop=True)
                mm.then_inc(first_sum, 1)

        @block.scalar
        def _(act):
            act.wait_ge(c_out_of_psum, 1)
            act.activation(CC[:, :], CC[:, :], ACT.Silu).then_inc(c_act, 1)
            act.wait_ge(lb_step, 2)
            act.activation(LBW[:, 0:2, :], LBW[:, 0:2, :], ACT.Exp).then_inc(lb_exp, 1)

        @block.vector
        def _(dve):
            dve.memset(EPSC[:, :], EPS).then_inc(eps_set, 1)
            dve.wait_ge(const_in, 32)
            dve.tensor_scalar(LM[:, :, :], LMF[:, :].rearrange("p (v r) -> p v r", v=A_LEVELS),
                              0.0, None, ALU.is_gt).then_inc(mask_set, 1)
            dve.memset(LB[:, :, :], 0.0).then_inc(lb_step, 1)
            dve.wait_ge(c_turned, 1)
            dve.tensor_copy(CC[:, :], PS[:, 0, 0:8])
            dve.tensor_copy(LBW[:, 0:2, :], PS[:, 0, 8:20].rearrange("p (l h) -> p l h", l=2)).then_inc(c_out_of_psum, 1)
            dve.wait_ge(c_out_of_psum, 1)
            dve.tensor_tensor(LBW[:, 2, :], LBW[:, 0, :], LBW[:, 1, :], ALU.max).then_inc(lb_part, 1)
            dve.wait_ge(lb_part, 1)
            dve.tensor_tensor(LBW[:, 0:2, :], LBW[:, 0:2, :],
                              LBW[:, 2:3, :].broadcast_to([P, 2, A_HEADS]), ALU.subtract).then_inc(lb_step, 1)
            for k in range(KT):
                dve.wait_ge(x_turned, k + 1)
                dve.tensor_copy(X[:, k, :], PS[:, 1 + k % 2, :]).then_inc(x_out, 1)
                if k == 1:
                    dve.wait_ge(lb_exp, 1)
                    dve.tensor_tensor(LBW[:, 2, :], LBW[:, 0, :], LBW[:, 1, :], ALU.add).then_inc(lb_part, 1)
                    dve.wait_ge(lb_part, 2)
                    dve.reciprocal(LBW[:, 3, :], LBW[:, 2, :]).then_inc(lb_part, 1)
                    dve.wait_ge(lb_part, 3)
                    dve.tensor_tensor(LB[:, 1, :], LBW[:, 1, :], LBW[:, 3, :], ALU.mult).then_inc(lb_part, 1)
            dve.wait_ge(cols_turned, DEPTH)
            for l in range(DEPTH):
                dve.tensor_copy(COLS[:, l, :], PS[:, 3, l * P:l * P + 120]).then_inc(cols_out, 1)
            dve.wait_ge(c_act, 1)
            for ch in range(ADA_FIRST + 1):
                for k in range(KT if ch < ADA_FIRST else 0):
                    acc, w = AACC[ch % 2][:, :], AWB[ch % 2][:, k, :]
                    if k == 0:
                        dve.wait_ge(first_in[ch % 2], 16 * (ch // 2 + 1))
                        ins = dve.tensor_scalar(acc, w, CC[:, k:k + 1], None, ALU.mult)
                    else:
                        dve.wait_ge(first_part, KT * ch + k)
                        ins = dve.scalar_tensor_tensor(acc, w, CC[:, k:k + 1], acc, ALU.mult, ALU.add)
                    ins.then_inc(first_part, 1)
                if ch:
                    dve.wait_ge(first_sum, ch)
                    dve.tensor_copy(MOD[:, 4 * ch - 4:4 * ch], PS[:, 5 - ch % 2, 0:4]).then_inc(first_out, 1)

    with nc.Fori(0, DEPTH) as l:
        with nc.Block() as block:
            @block.sync
            def _(sp):
                def of_layer(name):
                    return t[name][bass.ds(l, 1)]

                sp.dma_start(NGR[:, :], of_layer("hgrn_norm_g").broadcast_to([P, A_V])).then_inc(ngr_in, 16)
                def load(g, pieces):
                    sp.wait_ge(w_low, max(g - 1, 0))
                    for dst, src in pieces:
                        sp.dma_start(dst, src).then_inc(loaded[g % 2], 16)

                def ffn(f, g0, name, g1, name_out):
                    w = of_layer(name).rearrange("o (k p) (h c) -> p (o k) h c", p=P, h=2)
                    w_ada = t["w_ada"][bass.ds(l if f == 0 else l * -1 + (DEPTH - 1), 1)].rearrange(
                        "o (k p) c -> p (o k) c", p=P)
                    ch0 = (ADA_FIRST, 0)[f]

                    def raw(u):
                        return RAW[(g0 + u) % 2][:, :].rearrange("p (k h c) -> p k h c", k=KT, h=2)

                    def pieces(i, u, times):
                        for k in range(4 * u, 4 * u + 4):
                            sp.wait_ge(ada_part, i * KT + ((ADA_BEFORE[f] + 1) * KT + k - 1))
                            sp.dma_start(
              AW[k % 2][:, :], w_ada[:, k, bass.ds(i * SEQ + ch0 * SEQ, SEQ)]).then_inc(ada_in[k % 2], 16)

                    for u in range(2):
                        load(g0 + u, [(raw(u)[:, :, h, :], w[:, :, h, u * P:(u + 1) * P]) for h in range(2)])
                    def next_group(i, u, times):
                        sp.wait_ge(w_low, i * 2 + (g0 + u + 1))
                        for h in range(2):
                            sp.dma_start(raw(u)[:, :, h, :], w[:, :, h, bass.ds(i * 2 * P + (u + 2) * P, P)]).then_inc(loaded[(g0 + u) % 2], 16)

                    last, both = FI // 2 - 1, min(ADA_CHUNKS[f], FI // 2 - 1)
                    with sp.Fori(0, both) as i:
                        for u in range(2):
                            pieces(i, u, both)
                            next_group(i, u, both)
                    if ADA_CHUNKS[f] > last:
                        for u in range(2):
                            pieces(last, u, 1)
                            row_groups(g1, name_out, u, u + 1)
                    else:
                        with sp.Fori(both, last) as i:
                            for u in range(2):
                                next_group(i, u, last - both)
                        row_groups(g1, name_out, 0, 2)
                    row_groups(g1, name_out, 2, FO)

                def row_groups(g0, name, i0, i1):
                    w = of_layer(name).rearrange("o (g k p) c -> p (o g) k c", p=P, k=2)
                    for i in range(i0, i1):
                        raw = RAW[(g0 + i) % 2][:, :].rearrange("p (k c) -> p k c", k=2)
                        load(g0 + i, [(raw[:, k, :], w[:, i, k, :]) for k in range(2)])

                ffn(0, G_FFN1, "ffn1_w_in", G_FO1, "ffn1_w_out")
                w = of_layer("w_in").rearrange("o (k p) c -> p (o k) c", p=P)
                for m, (kind, c0, c1) in enumerate(MIX):
                    raw = RAW[(G_MIX + m) % 2]
                    if kind in PAIR_KINDS:
                        v = raw[:, :].rearrange("p (k h c) -> p k h c", k=KT, h=2)
                        load(G_MIX + m, [(v[:, :, h, :], w[:, :, c:c + P]) for h, c in enumerate((c0, c1))])
                    else:
                        v = raw[:, 0:KT * c1].rearrange("p (k c) -> p k c", k=KT)
                        load(G_MIX + m, [(v[:, k:k + 4, :], w[:, k:k + 4, c0:c0 + c1]) for k in (0, 4)])
                for i in range(4):
                    raw = RAW[(G_BR + i) % 2][:, :].rearrange("p (k c) -> p k c", k=KT)
                    load(G_BR + i, [(raw[:, k0:k0 + n, :],
                                     of_layer(name).rearrange("o (k p) c -> p (o k) c", p=P)[:, :, 256 * i:256 * i + 256])
                                    for name, k0, n in (("w_branch_a", 0, 3), ("w_branch_b", 3, 3), ("w_branch_c", 6, 2))])
                row_groups(G_WO, "w_out", 0, 4)
                ffn(1, G_FFN2, "ffn2_w_in", G_FO2, "ffn2_w_out")

            @block.tensor
            def _(pe):
                def three(o, ah, al, bh, bl, start, stop):
                    pe.matmul(o, ah, bh, start=start, stop=False)
                    pe.matmul(o, ah, bl, start=False, stop=False)
                    return pe.matmul(o, al, bh, start=False, stop=stop)

                def norm_sum(n, q):
                    pe.wait_ge(n_ss, 4 * n + q + 1)
                    pe.matmul(PS[:, 1 - n % 2, :], ones, NSS[q % 2][:, :], start=(q == 0), stop=(q == 3)).then_inc(n_mm, 1)

                def input_tile(s, k):
                    pe.wait_ge((h_low_even, h_low_odd)[k % 2], 4 * s + k // 2 + 1)

                def ffn_in(s, f, g0):
                    def group(u, times):
                        wh = WH[(g0 + u) % 2][:, :].rearrange("p (k h c) -> p k h c", k=KT, h=2)
                        wl = WL[(g0 + u) % 2][:, :].rearrange("p (k h c) -> p k h c", k=KT, h=2)
                        for half in range(2):
                            for k in range(KT):
                                mm = three(PS[:, 2 * u + half, :], wh[:, k, half, :], wl[:, k, half, :],
                                           HH[:, k, :], HL[:, k, :], k == 0, k == KT - 1)
                            mm.then_inc((a_done, w_used)[half], 1)

                    pe.wait_ge(w_low, g0 + 2)
                    w4 = [[w[(g0 + u) % 2][:, :].rearrange("p (k h c) -> p k h c", k=KT, h=2) for w in (WH, WL)]
                          for u in range(2)]
                    for k in range(KT):
                        input_tile(s, k)
                        for u in range(2):
                            for half in range(2):
                                mm = three(PS[:, 2 * u + half, :], w4[u][0][:, k, half, :], w4[u][1][:, k, half, :],
                                           HH[:, k, :], HL[:, k, :], k == 0, k == KT - 1)
                                if k == KT - 1:
                                    mm.then_inc((a_done, w_used)[half], 1)

                    def ada(i, times=1):
                        pe.wait_ge(ada_part, i * KT + (ADA_BEFORE[f] + 2) * KT)
                        for q in range(4):
                            mm = pe.matmul(PS[:, 4, q:q + 1], AACC[0][:, q * P:(q + 1) * P], ones[:, 0:1],
                                           start=True, stop=True)
                        mm.then_inc(ada_sum, 1)

                    ada(0)
                    for first, end in ((1, ADA_CHUNKS[f]), (ADA_CHUNKS[f], FI // 2)):
                        if first < end:
                            times = end - first
                            with pe.Fori(first, end) as i:
                                for u in range(2):
                                    pe.wait_ge(w_low, i * 2 + (g0 + u + 1))
                                    pe.wait_ge(gated, i * 2 + (FT * f + u - 1))
                                    group(u, times)
                                if end == ADA_CHUNKS[f]:
                                    ada(i, times)

                def rows_product(g0, n, rh, rl, ready, s):
                    for i in range(n):
                        pe.wait_ge(w_low, g0 + i + 1)
                        ready(i)
                        wh = WH[(g0 + i) % 2][:, :].rearrange("p (k c) -> p k c", k=2)
                        wl = WL[(g0 + i) % 2][:, :].rearrange("p (k c) -> p k c", k=2)
                        for j in range(KT):
                            for k in range(2):
                                mm = three(PS[:, j, :], wh[:, k, j * P:(j + 1) * P], wl[:, k, j * P:(j + 1) * P],
                                           rh(2 * i + k), rl(2 * i + k), i == 0 and k == 0, i == n - 1 and k == 1)
                            if i == n - 1:
                                mm.then_inc(y_done, 1)
                                if j in (3, 5, 7):
                                    norm_sum(2 * s + 1, (j - 3) // 2)
                            elif j == KT - 1:
                                mm.then_inc(w_used, 1)

                def ffn_out(s, f, g0):
                    def ready(i):
                        if i == 0:
                            pe.wait_ge(gated, FT * (f + 1))
                            pe.wait_ge(ada_out, (ADA_CHUNKS[0], ADA_ALL)[f])
                        pe.wait_ge(g_low, FT * f + 2 * i + 2)
                    rows_product(g0, FO, lambda k: GH[:, k, :], lambda k: GL[:, k, :], ready, s)

                def project(m, k):
                    kind, c0, c1 = MIX[m]
                    slot = (G_MIX + m) % 2
                    if k == 0:
                        pe.wait_ge(w_low, G_MIX + m + 1)
                    if m == 0:
                        wh, wl = (w[slot][:, :].rearrange("p (k h c) -> p k h c", k=KT, h=2) for w in (WH, WL))
                        input_tile(1, k)
                        for i in range(2):
                            mm = three(PS[:, i, :], wh[:, k, i, :], wl[:, k, i, :], HH[:, k, :], HL[:, k, :], k == 0, k == 7)
                            if k == 7:
                                mm.then_inc((tile_done, w_used)[i], 1)
                        return
                    if kind in TOKEN_KINDS:
                        i, k0, nk, width = k // 2, 4 * (k % 2), 4, c1
                        wh = WH[slot][:, 0:KT * width].rearrange("p (k c) -> p k c", k=KT)
                        wl = WL[slot][:, 0:KT * width].rearrange("p (k c) -> p k c", k=KT)
                    else:
                        i, k0, nk, width = k // 4, 2 * (k % 4), 2, SEQ
                        wh = WH[slot][:, :].rearrange("p (k h c) -> p k h c", k=KT, h=2)
                        wl = WL[slot][:, :].rearrange("p (k h c) -> p k h c", k=KT, h=2)
                    tile = TILE0[m] + i
                    if k0 == 0:
                        pe.wait_ge(tile_out[tile % 2], tile // 2)
                    o = PS[:, tile % 2, 0:width]
                    for kk in range(k0, k0 + nk):
                        if kind in TOKEN_KINDS:
                            tok = slice(i, SEQ, 4) if kind == "cv" and c0 > COL_CV else slice(i * P, (i + 1) * P)
                            mm = three(o, HH[:, kk, tok], HL[:, kk, tok], wh[:, kk, :], wl[:, kk, :], kk == 0, kk == KT - 1)
                        else:
                            mm = three(o, wh[:, kk, i, :], wl[:, kk, i, :], HH[:, kk, :], HL[:, kk, :], kk == 0, kk == KT - 1)
                    if k0 + nk == KT:
                        mm.then_inc(w_used if k == 7 else tile_done, 1)

                def a_head(h, k):
                    aq, ab, ak = AQ[h % 2], AB[h % 2], AK[h % 2]
                    if k == 0:
                        pe.wait_ge(p_k, h + 1)
                        pe.wait_ge(p_q, h + 1)
                        pe.wait_ge(i_s0, h)
                        for c in range(TT):
                            mm = pe.matmul(PS[:, 4, c * P:(c + 1) * P], ak[:, c * P:(c + 1) * P], aq[:, c * P:(c + 1) * P],
                                           start=True, stop=True)
                        mm.then_inc(i_diag, 1)
                    if k:
                        n = A_LEVELS * h + k - 1
                        pe.wait_ge(v_scaled, n + 1)
                        pe.wait_ge(v_out, max(n - 1, 0))
                        for c in range(TT):
                            mm = pe.matmul(PS[:, 2 + n % 2, c * 64:(c + 1) * 64], KL[n % 2][:, c * P:(c + 1) * P],
                                           QL[n % 2][:, c, :], start=True, stop=True)
                        mm.then_inc(v_mm, 1)
                    if k == 3:
                        pe.wait_ge(i_kd, h + 1)
                        pe.wait_ge(i_kdt, h)
                        for c in range(TT - 1):
                            mm = pe.transpose(PS[:, 5, c * P:(c + 1) * P], KD[:, c * P:(c + 1) * P], ident)
                        mm.then_inc(i_turn, 1)
                    if k == 5:
                        pe.wait_ge(i_kdt, h + 1)
                        pe.wait_ge(i_st, 3 * h)
                        for c in range(TT - 1):
                            mm = pe.matmul(PS[:, 6, c * A_V:(c + 1) * A_V], KDT[:, c, :], AV[:, c, h * A_V:(h + 1) * A_V],
                                           start=True, stop=True)
                        mm.then_inc(i_u, 1)

                def a_output(h):
                    pe.wait_ge(v_out, A_LEVELS * (h + 1))
                    pe.wait_ge(i_qb, h + 1)
                    pe.wait_ge(i_st, 3 * h + 3)
                    pe.wait_ge(i_oout, h)
                    for c in range(TT):
                        o = PS[:, 7, c * A_V:(c + 1) * A_V]
                        mm = pe.matmul(o, AS[h % 2][:, c, :], AV[:, c, h * A_V:(h + 1) * A_V], start=True, stop=(c == 0))
                        if c:
                            mm = pe.matmul(o, QB[h % 2][:, c * P:(c + 1) * P], ST[h % 2][:, c - 1, :], start=False, stop=True)
                    mm.then_inc(i_o, 1)

                def b_scores(h):
                    pr = slice((h % 2) * HD, (h % 2) * HD + HD)
                    pe.wait_ge(*taken(TILE0[ITEM_B + h // 2] + 1))
                    if h == 0:
                        pe.wait_ge(i_oout, A_HEADS)
                    pe.wait_ge(b_out, max(h - 1, 0))
                    for i in (0, 1, 3, 2):
                        bank, col = z_at(i, h)
                        mm = pe.matmul(PS[:, bank, col:col + zw(i)], BK[h // 2 % 2][pr, i * P:(i + 1) * P],
                                       BQ[h // 2 % 2][pr, i * P:SEQ], start=(i != 3), stop=True, skip_group_check=True)
                    mm.then_inc(b_z, 1)

                def b_args(h):
                    pe.wait_ge(b_spm, h + 1)
                    for i in range(TT):
                        bank, col = z_at(i, h)
                        mm = pe.matmul(PS[:, bank, col:col + P], ident, const("negm"), start=False, stop=True, skip_group_check=True)
                        mm = pe.matmul(PS[:, bank, col:col + zw(i)], const("ntri"), BS[h % 2][:, ZCOL[i]:ZCOL[i] + zw(i)],
                                       start=False, stop=True, skip_group_check=True)
                        for j in range(i + 1, TT):
                            mm = pe.matmul(PS[:, bank, col + P * (j - i):col + zw(i)], const("nones"),
                                           BS[h % 2][:, ZCOL[j]:ZCOL[j] + zw(j)], start=False, stop=True, skip_group_check=True)
                    mm.then_inc(b_arg, 1)

                def b_values(h):
                    pe.wait_ge(b_a, h + 1)
                    for j in range(TT):
                        for i in range(j + 1):
                            a = ZCOL[i] + P * (j - i)
                            mm = pe.matmul(PS[:, 4 + 3 * (h % 2), 256 + j * HD:256 + (j + 1) * HD], BA[h % 2][:, a:a + P],
                                           BV[:, i, h * HD:(h + 1) * HD], start=(i == 0 and j == 0), stop=True,
                                           skip_group_check=True)
                    mm.then_inc(b_pv, 1)

                def c_scores(n):
                    h, t0 = units[n]
                    pair, pr = h // 2, slice((h % 2) * HD, (h % 2) * HD + HD)
                    pe.wait_ge(*taken(TILE0[ITEM_C + pair] + 1))
                    if n == 0:
                        pe.wait_ge(b_out, B_HEADS)
                    pe.wait_ge(c_bias, max(n - 1, 0))
                    for q in range(4):
                        tq, tk = (t0 + q // 2, max(t0 + q // 2 - 1 + q % 2, 0)) if h < C_SLOTS else (q, q)
                        mm = pe.matmul(PS[:, 2 + n % 2, q * P:(q + 1) * P], CQ[pair % 2][pr, tq * P:(tq + 1) * P],
                                       CK[pair % 2][pr, tk * P:(tk + 1) * P], start=True, stop=True)
                    mm.then_inc(c_s, 1)

                def c_turn(n):
                    pe.wait_ge(c_p, n + 1)
                    pe.wait_ge(c_pt, max(n - 1, 0))
                    for q in range(4):
                        mm = pe.transpose(PS[:, 4 + n % 2, q * P:(q + 1) * P], CP[n % 2][:, q * P:(q + 1) * P], ident)
                    mm.then_inc(c_t, 1)

                def c_values(n):
                    h, t0 = units[n]
                    if n == 0:
                        pe.wait_ge(*taken(TILE0[ITEM_C] - 1))
                        pe.wait_ge(*taken(TILE0[ITEM_C] - 2))
                        pe.wait_ge(c_ones, 1)
                    pe.wait_ge(c_pt, n + 1)
                    pe.wait_ge(c_out, max(n - 1, 0))
                    for q in range(4):
                        first, last = (q % 2 == 0, q % 2 == 1) if h < C_SLOTS else (True, True)
                        o, tk = (q // 2, max(t0 + q // 2 - 1 + q % 2, 0)) if h < C_SLOTS else (q, q)
                        mm = pe.matmul(PS[:, 6 + n % 2, o * 65:(o + 1) * 65], CPT[n % 2][:, q * P:(q + 1) * P], CV[:, tk, h, :],
                                       start=first, stop=last)
                    mm.then_inc(c_pv, 1)

                def turn_mixed(ft):
                    if ft == 0:
                        pe.wait_ge(an, 5)
                        pe.wait_ge(b_out, B_HEADS)
                        pe.wait_ge(cmb, 10)
                    pe.wait_ge(yt_low, max(ft - 3, 0))
                    src, c = (OA, ft) if ft < 3 else (OB, ft - 3) if ft < 6 else (OF, ft - 6)
                    for i in range(TT):
                        mm = pe.transpose(PS[:, 2 + ft % 4, i * P:(i + 1) * P], src[:, i, c * P:(c + 1) * P], ident)
                    mm.then_inc(yt_done, 1)

                def mixers(m, k):
                    if m % 2 == 0 and 0 < m <= 2 * A_HEADS:
                        a_head(m // 2 - 1, k)
                    if m % 2 and 3 <= m <= 2 * A_HEADS + 1 and k == 2:
                        a_output((m - 3) // 2)
                    hb = 2 * (m - (ITEM_B + 2)) + k // 4
                    if k % 4 == 0 and 0 <= hb < B_HEADS:
                        b_scores(hb)
                    if k % 4 == 1 and 1 <= hb <= B_HEADS:
                        b_args(hb - 1)
                    if k % 4 == 3 and 1 <= hb <= B_HEADS:
                        b_values(hb - 1)
                    if (m, k) in UNIT_AT:
                        n = UNIT_AT[(m, k)]
                        if n < NU:
                            c_scores(n)
                        if 1 <= n <= NU:
                            c_turn(n - 1)
                        if 2 <= n:
                            c_values(n - 2)
                    if m >= ITEM_TURN and k % 4 == 0 and 2 * (m - ITEM_TURN) + k // 4 < KT:
                        turn_mixed(2 * (m - ITEM_TURN) + k // 4)

                def merge():
                    pe.wait_ge(yt_low, KT)
                    pe.wait_ge(*taken(NTILES - 1))
                    pe.wait_ge(*taken(NTILES - 2))
                    for q in range(4):
                        pe.wait_ge(w_low, G_BR + q + 1)
                        wh = WH[(G_BR + q) % 2][:, :].rearrange("p (k c) -> p k c", k=KT)
                        wl = WL[(G_BR + q) % 2][:, :].rearrange("p (k c) -> p k c", k=KT)
                        for u in range(2):
                            j = 2 * q + u
                            pe.wait_ge(br_mul, max(j - 1, 0))
                            for n, (k0, k1) in enumerate(((0, 3), (3, 6), (6, 8))):
                                for k in range(k0, k1):
                                    mm = three(PS[:, 3 * (j % 2) + n, :], wh[:, k, u * P:(u + 1) * P], wl[:, k, u * P:(u + 1) * P],
                                               YH[k][:, :], YL[k][:, :], k == k0, k == k1 - 1)
                            mm.then_inc((br_done, w_used)[u], 1)

                def norms(s):
                    norm_sum(2 * s + 1, 3)
                    if s < 2:
                        for q in range(4):
                            norm_sum(2 * s + 2, q)

                for q in range(4):
                    norm_sum(0, q)
                ffn_in(0, 0, G_FFN1)
                ffn_out(0, 0, G_FO1)
                norms(0)
                for m in range(NM):
                    for k in range(8):
                        project(m, k)
                        mixers(m, k)
                merge()

                def merged(i):
                    if i == 0:
                        pe.wait_ge(br_mul, KT)
                    pe.wait_ge(m_low, 2 * i + 2)
                rows_product(G_WO, 4, lambda k: HH[:, k, :], lambda k: HL[:, k, :], merged, 1)
                norms(1)
                ffn_in(2, 1, G_FFN2)
                ffn_out(2, 1, G_FO2)
                norms(2)

            @block.scalar
            def _(act):
                def high(g):
                    slot = g % 2
                    act.wait_ge(loaded[slot], 16 * loads_until(g))
                    if g >= 2:
                        act.wait_ge(*used(g - 2))
                    n = group_columns(g)
                    act.activation(WH[slot][:, 0:n], RAW[slot][:, 0:n], ACT.Copy).then_inc(w_high, 1)

                def high_part(m, q):
                    g = G_MIX + m
                    slot, n = g % 2, group_columns(g) // 4
                    if q == 0:
                        act.wait_ge(loaded[slot], 16 * loads_until(g))
                        act.wait_ge(*used(g - 2))
                    act.activation(WH[slot][:, q * n:(q + 1) * n], RAW[slot][:, q * n:(q + 1) * n], ACT.Copy).then_inc(w_high if q == 3 else part_high, 1)

                def norm(n, square):
                    for q in range(4):
                        act.wait_ge(n_ss, 4 * n + max(q - 1, 0))
                        square(q)
                    act.wait_ge(n_mm, 4 * n + 4)
                    act.activation(NLN[:, :], PS[:, 1 - n % 2, :], ACT.Ln, bias=EPSC[:, 0:1], scale=1.0 / D).then_inc(n_ln, 1)
                    act.wait_ge(n_ln, n + 1)
                    act.activation(NR[:, :], NLN[:, :], ACT.Exp, scale=-0.5).then_inc(n_r, 1)

                def post(s):
                    def square(q):
                        for i in range(2):
                            act.wait_ge(y_done, KT * s + 2 * q + i + 1)
                            act.activation(NSQ[q % 2][:, i, :], PS[:, 2 * q + i, :], ACT.Square).then_inc(n_sq, 1)
                    act.preload_act_table_set("natural_log_exp_and_others")
                    norm(2 * s + 1, square)

                def pre(s):
                    def square(q):
                        for i in range(2):
                            if s:
                                act.wait_ge((x_even, x_odd)[i], 4 * (s - 1) + q + 1)
                            act.activation(NSQ[q % 2][:, i, :], X[:, 2 * q + i, :], ACT.Square).then_inc(n_sq, 1)
                    if s == 0:
                        act.preload_act_table_set("natural_log_exp_and_others")
                    norm(2 * s, square)

                def inputs(s):
                    for j in range(KT):
                        act.wait_ge(u_done, KT * s + j + 1)
                        act.activation(HH[:, j, :], U[:, j, :], ACT.Identity, bias=MOD[:, 24 * s + j:24 * s + j + 1]).then_inc(h_high, 1)

                def ffn_in(f, g0):
                    act.preload_act_table(ACT.Silu)
                    with act.Fori(0, FI // 2) as i:
                        for u in range(2):
                            slot, times = (g0 + u) % 2, FI // 2
                            act.wait_ge(a_done, i * 2 + (FT * f + u + 1))
                            if u:
                                act.wait_ge(g_low, i * 2 + (FT * f + 1))
                            act.activation(SB[u][:, :], PS[:, 2 * u, :], ACT.Silu).then_inc(silu_done, 1)
                            act.wait_ge(w_used, i * 2 + used_count(g0 + u))
                            act.wait_ge(loaded[slot], i * 32 + 16 * loads_until(g0 + u + 2))
                            act.activation(WH[slot][:, :], RAW[slot][:, :], ACT.Copy).then_inc(w_high, 1)
                            act.wait_ge(gated, i * 2 + (FT * f + u + 1))
                            act.activation(GH[:, bass.ds(i * 2 + u, 1), :].rearrange("p o c -> p (o c)"),
                                           SB[u][:, :], ACT.Copy).then_inc(g_high, 1)

                def row_groups(g0, n):
                    for i in range(n):
                        if g0 + i + 2 < NG:
                            high(g0 + i + 2)

                def a_prepare(h, k):
                    if k == 0:
                        act.wait_ge(*taken(TILE0[2 * h]))
                        act.wait_ge(*taken(TILE0[2 * h] + 1))
                        act.wait_ge(p_mask, h)
                        act.wait_ge(p_log, 3 * h)
                        act.activation(W1[:, :, :], QF[:, :, :], ACT.Abs).then_inc(p_abs, 1)
                        act.wait_ge(p_abs, h + 1)
                        act.activation(W1[:, :, :], W1[:, :, :], ACT.Exp, scale=-1.0).then_inc(p_e, 1)
                        act.wait_ge(p_e, h + 1)
                        act.activation(W1[:, :, :], W1[:, :, :], ACT.Ln, bias=1.0).then_inc(p_ln, 1)
                    if k == 2:
                        act.wait_ge(p_t, h + 1)
                        act.activation(W2[:, :, :], W2[:, :, :], ACT.Exp).then_inc(p_sg, 1)
                        act.activation(AK[h % 2][:, :], AK[h % 2][:, :], ACT.Exp).then_inc(p_sn, 1)
                    if k == 3:
                        act.wait_ge(p_sn, h + 1)
                        act.activation(AK[h % 2][:, :], AK[h % 2][:, :], ACT.Copy, scale=OML[:, h:h + 1]).then_inc(p_k, 1)
                    if k == 5:
                        act.wait_ge(p_f, 3 * h + 3)
                        act.wait_ge(v_diff, A_LEVELS * max(h - 1, 0))
                        act.wait_ge(i_diff, max(h - 1, 0))
                        act.activation(AB[h % 2][:, :], W1[:, 0, :], ACT.Ln).then_inc(p_lf, 1)
                        act.activation(W1[:, 1, :], W1[:, 1, :], ACT.Ln, scale=LN_LIFT).then_inc(p_lf, 1)

                def a_head(h, k):
                    if k == 0:
                        act.wait_ge(p_log, 3 * h + 3)
                        act.wait_ge(i_qb, h)
                        act.wait_ge(i_st, 3 * h)
                        act.activation(EB[:, :], AB[h % 2][:, :], ACT.Exp).then_inc(i_eb, 1)
                    if k == 4:
                        act.wait_ge(i_turn, h + 1)
                        act.activation(KDT[:, :, :], PS[:, 5, 0:384].rearrange("p (c t) -> p c t", c=3), ACT.Copy).then_inc(i_kdt, 1)
                    if k == 1:
                        act.wait_ge(i_diff, h + 1)
                        act.activation(KD[:, :], KD[:, :], ACT.Exp, scale=-1.0).then_inc(i_decay, 1)
                    if k < A_LEVELS:
                        n = A_LEVELS * h + k
                        act.wait_ge(v_diff, n + 1)
                        act.wait_ge(v_scaled, max(n - 1, 0))
                        act.activation(level_view(AE[n % 2][:, :], k, 0), level_view(AD[n % 2][:, :], k, 0), ACT.Exp, scale=-1.0)
                        act.activation(level_view(AE[n % 2][:, :], k, 1), level_view(AD[n % 2][:, :], k, 1), ACT.Exp).then_inc(v_decay, 1)

                def take_a(m, i):
                    tile = TILE0[m] + i
                    act.wait_ge(*projected(m, i))
                    act.wait_ge((p_q, p_t)[i], m // 2)
                    act.activation(QF[:, i, :], PS[:, tile % 2, :], ACT.Copy).then_inc(tile_out[tile % 2], 1)

                def a_norm():
                    act.wait_ge(an, 2)
                    act.activation(ARS[:, 1, :], ARS[:, 0, :], ACT.Ln, bias=EPSC[:, 0:1], scale=1.0 / A_V).then_inc(an_ln, 1)
                    act.wait_ge(an_ln, 1)
                    act.activation(ARS[:, 2, :], ARS[:, 1, :], ACT.Exp, scale=-0.5).then_inc(an_r, 1)

                def gates_silu():
                    act.wait_ge(*taken(TILE0[8] - 1))
                    act.wait_ge(*taken(TILE0[8] - 2))
                    act.activation(GN[:, :, :], GN[:, :, :], ACT.Silu).then_inc(gn_silu, 1)
                    act.preload_act_table_set("natural_log_exp_and_others")

                def b_softplus(h):
                    act.wait_ge(b_z, h + 1)
                    act.wait_ge(b_sp, max(h - 1, 0))
                    s = 3 * (h % 2)
                    z = BZ[h % 2]
                    act.activation(z[:, 0:512], PS[:, 2 + s, :], ACT.Abs)
                    act.activation(z[:, 512:1024], PS[:, 3 + s, :], ACT.Abs)
                    act.activation(z[:, 1024:1280], PS[:, 4 + s, 0:256], ACT.Abs).then_inc(b_abs, 1)
                    act.wait_ge(b_abs, h + 1)
                    act.activation(z[:, :], z[:, :], ACT.Exp, scale=-1.0).then_inc(b_e, 1)
                    act.wait_ge(b_e, h + 1)
                    act.activation(z[:, :], z[:, :], ACT.Ln, bias=1.0).then_inc(b_ln, 1)

                def b_weights(h):
                    act.wait_ge(b_arg, h + 1)
                    act.wait_ge(b_pv, max(h - 1, 0))
                    s = 3 * (h % 2)
                    a = BA[h % 2]
                    act.activation(a[:, 0:512], PS[:, 2 + s, :], ACT.Exp)
                    act.activation(a[:, 512:1024], PS[:, 3 + s, :], ACT.Exp)
                    act.activation(a[:, 1024:1280], PS[:, 4 + s, 0:256], ACT.Exp).then_inc(b_a, 1)

                def c_unit(n):
                    if n < NU:
                        act.wait_ge(c_sub, n + 1)
                        act.wait_ge(c_t, max(n - 1, 0))
                        act.activation(CP[n % 2][:, :], CS[n % 2][:, :], ACT.Exp).then_inc(c_p, 1)
                    if 1 <= n <= NU:
                        act.wait_ge(c_t, n)
                        act.wait_ge(c_pv, max(n - 2, 0))
                        act.activation(CPT[(n - 1) % 2][:, :], PS[:, 4 + (n - 1) % 2, :], ACT.Copy).then_inc(c_pt, 1)

                def to_token_order():
                    act.wait_ge(c_out, NU)
                    for c in range(4):
                        for j in range(TT):
                            act.dma_start(OCN[c:P:4, j, :, :], OC[32 * j:32 * j + 32, c, 4:12, :]).then_inc(c_perm, 16)

                def mixers(m, k):
                    if k == 0 and m and MIX[m - 1][0] == "a":
                        if m == 1:
                            take_a(m - 1, 0)
                        take_a(m - 1, 1)
                    if k == 4 and m and MIX[m][0] == "a":
                        take_a(m, 0)
                    if m % 2 == 0 and 0 < m <= 2 * A_HEADS:
                        a_head(m // 2 - 1, k)
                    if m % 2 and m < 2 * A_HEADS:
                        a_prepare(m // 2, k)
                    if (m, k) == (ITEM_B + 1, 0):
                        gates_silu()
                    if (m, k) == (ITEM_B + 1, 5):
                        a_norm()
                    hb = 2 * (m - (ITEM_B + 2)) + k // 4
                    if k % 4 == 0 and 0 <= hb < B_HEADS:
                        b_softplus(hb)
                    if k % 4 == 1 and 1 <= hb <= B_HEADS:
                        b_weights(hb - 1)
                    if (m, k) in UNIT_AT:
                        c_unit(UNIT_AT[(m, k)])
                    if (m, k) == (ITEM_COMBINE - 1, 0):
                        to_token_order()
                    if (m, k) == (ITEM_COMBINE, 2):
                        act.wait_ge(cmb, 5)
                        act.activation(CW[:, 1:4, :], CW[:, 1:4, :], ACT.Exp).then_inc(cmb_e, 1)
                    if m >= ITEM_TURN and k % 4 == 2 and 2 * (m - ITEM_TURN) + k // 4 < KT:
                        ft = 2 * (m - ITEM_TURN) + k // 4
                        act.wait_ge(yt_done, ft + 1)
                        act.activation(YH[ft][:, :], PS[:, 2 + ft % 4, :], ACT.Copy).then_inc(yt_high, 1)

                def gate_sigmoids(i0, i1):
                    for i in range(i0, i1):
                        act.wait_ge(*taken(TILE0[ITEM_GATE] + i))
                        act.activation(GT[i][:, :], GT[i][:, :], ACT.Sigmoid).then_inc(g_sig, 1)

                high(0)
                high(1)
                pre(0)
                inputs(0)
                ffn_in(0, G_FFN1)
                row_groups(G_FO1, FO - 1)
                post(0)
                high(G_MIX + 1)
                pre(1)
                inputs(1)
                for m in range(NM):
                    for k in range(8):
                        if 1 <= k <= 4 and m:
                            if m + 1 < NM:
                                high_part(m + 1, k - 1)
                            elif k == 1:
                                high(G_BR)
                        mixers(m, k)
                        if m >= ITEM_TURN and k == 7:
                            gate_sigmoids(3 * (m - ITEM_TURN), min(3 * (m - ITEM_TURN) + 3, 23))
                gate_sigmoids(23, 24)
                high(G_BR + 1)
                for q in range(4):
                    for u in range(2):
                        j = 2 * q + u
                        act.wait_ge(br_sum, j + 1)
                        act.activation(HH[:, j, :], MA[j % 2][:, 0, :], ACT.Copy).then_inc(m_high, 1)
                    high(G_BR + q + 2)
                row_groups(G_WO, 3)
                post(1)
                high(G_WO + 5)
                pre(2)
                inputs(2)
                ffn_in(1, G_FFN2)
                row_groups(G_FO2, FO - 1)
                post(2)

            @block.vector
            def _(dve):
                dve.tensor_scalar(OML[:, :], LB[:, bass.ds(l, 1), :].rearrange("p o h -> p (o h)"),
                                  -1.0, 1.0, ALU.mult, ALU.add).then_inc(lb_out, 1)

                dve.tensor_copy(LBC[:, :], LB[:, bass.ds(l, 1), :].rearrange("p o h -> p (o h)")).then_inc(ada_part, KT)

                def columns(c0, c1, subs):
                    dve.tensor_tensor(MOD[:, c0:c1], MOD[:, c0:c1],
                                      COLS[:, bass.ds(l, 1), c0:c1].rearrange("p o c -> p (o c)"), ALU.add).then_inc(ada_cols, 1)
                    dve.wait_ge(ada_cols, 1 if c0 == 0 else 4)
                    mod = MOD[:, :].rearrange("p (s v k) -> p s v k", s=3, v=3)
                    gains = COLS[:, bass.ds(l, 1), 72:120].rearrange("p o (s u k) -> p (o s) u k", s=3, u=2)
                    for s in subs:
                        dve.scalar_tensor_tensor(PRE[:, s, :], mod[:, s, 1, :], 1.0, gains[:, s, 0, :],
                                                 ALU.add, ALU.mult).then_inc(ada_cols, 1)
                        dve.scalar_tensor_tensor(POST[:, s, :], mod[:, s, 2, :], 1.0 if s == 1 else 0.5,
                                                 gains[:, s, 1, :], ALU.mult, ALU.mult).then_inc(ada_cols, 1)

                columns(0, 4 * ADA_FIRST, (0,))
                dve.wait_ge(ada_cols, 3)

                def add_halves(n, q):
                    dve.wait_ge(n_sq, KT * n + 2 * q + 2)
                    dve.wait_ge(n_mm, 4 * n + max(q - 1, 0))
                    dve.tensor_tensor(NSS[q % 2][:, :], NSQ[q % 2][:, 0, :], NSQ[q % 2][:, 1, :], ALU.add).then_inc(n_ss, 1)

                def post(s):
                    for j in range(KT):
                        dve.wait_ge(n_sq, KT * (2 * s + 1) + j + 1)
                        dve.tensor_scalar(Y[:, j, :], PS[:, j, :], POST[:, s, j:j + 1], None, ALU.mult).then_inc(y_copied, 1)
                        if j % 2:
                            add_halves(2 * s + 1, j // 2)
                    dve.wait_ge(n_r, 2 * s + 2)
                    for j in range(KT):
                        dve.tensor_tensor(Y[:, j, :], Y[:, j, :], NR[:, :], ALU.mult).then_inc(y_scaled, 1)
                        if j % 2:
                            dve.wait_ge(y_scaled, KT * s + j + 1)
                            dve.tensor_tensor(X[:, j, :], X[:, j, :], Y[:, j, :], ALU.add).then_inc(x_odd, 1)
                            if j > 1 and s < 2:
                                add_halves(2 * s + 2, j // 2 - 1)

                def low_of_input(s, j):
                    dve.wait_ge(h_high, KT * s + j + 1)
                    dve.scalar_tensor_tensor(HL[:, j, :], U[:, j, :], MOD[:, 24 * s + j:24 * s + j + 1],
                                             HH[:, j, :].bitcast(F32), ALU.add, ALU.subtract).then_inc(h_low_even, 1)

                def pre(s):
                    for q in range(3 if s else 0, 4):
                        add_halves(2 * s, q)
                    dve.wait_ge(n_r, 2 * s + 1)
                    for j in range(KT):
                        dve.scalar_tensor_tensor(U[:, j, :], X[:, j, :], PRE[:, s, j:j + 1], NR[:, :],
                                                 ALU.mult, ALU.mult).then_inc(u_done, 1)
                        if j in (1, 3, 5, 7):
                            low_of_input(s, j - 1)

                def ffn_in(f, g0):
                    for first, end in ((0, ADA_CHUNKS[f]), (ADA_CHUNKS[f], FI // 2)):
                        if first < end:
                            with dve.Fori(first, end) as i:
                                ffn_pair(f, g0, i, end == ADA_CHUNKS[f], end - first)

                def ffn_pair(f, g0, i, ada, times):
                    for u in range(2):
                        if ada:
                            for k in range(4 * u, 4 * u + 4):
                                acc, w = AACC[0][:, :], AW[k % 2][:, :]
                                dve.wait_ge(ada_in[k % 2], i * (16 * KT // 2) + 16 * (ADA_BEFORE[f] * KT // 2 + k // 2 + 1))
                                if k == 0:
                                    ins = dve.tensor_scalar(acc, w, CC[:, k:k + 1], None, ALU.mult)
                                else:
                                    dve.wait_ge(ada_part, i * KT + ((ADA_BEFORE[f] + 1) * KT + k))
                                    ins = dve.scalar_tensor_tensor(acc, w, CC[:, k:k + 1], acc, ALU.mult, ALU.add)
                                ins.then_inc(ada_part, 1)
                        n = FT * f + u + 1
                        dve.wait_ge(silu_done, i * 2 + n)
                        dve.wait_ge(w_used, i * 2 + used_count(g0 + u))
                        dve.tensor_tensor(SB[u][:, :], SB[u][:, :], PS[:, 2 * u + 1, :], ALU.mult).then_inc(gated, 1)
                        dve.wait_ge(g_high, i * 2 + n)
                        gh = GH[:, bass.ds(i * 2 + u, 1), :].rearrange("p o c -> p (o c)")
                        gl = GL[:, bass.ds(i * 2 + u, 1), :].rearrange("p o c -> p (o c)")
                        dve.tensor_tensor(gl, SB[u][:, :], gh.bitcast(F32), ALU.subtract).then_inc(g_low, 1)
                    if ada:
                        dve.wait_ge(ada_sum, i + (ADA_BEFORE[f] + 1))
                        dve.tensor_copy(MOD[:, bass.ds(i * 4 + 4 * (ADA_FIRST, 0)[f], 4)], PS[:, 4, 0:4]).then_inc(ada_out, 1)

                def take(m, i):
                    kind, c0, width = MIX[m]
                    if kind == "a":
                        return
                    dve.wait_ge(*projected(m, i))
                    tile = TILE0[m] + i
                    ps = PS[:, tile % 2, :]
                    if kind == "av":
                        c = c0 - COL_AI
                        ins = dve.tensor_copy(AV[:, i, c:c + width], ps[:, 0:width])
                    elif kind == "ag":
                        c = c0 - COL_AG
                        ins = dve.tensor_copy(GN[:, i, c:c + width], ps[:, 0:width])
                    elif kind == "bv":
                        c = c0 - COL_BV
                        ins = dve.tensor_copy(BV[:, i, c:c + width], ps[:, 0:width])
                    elif kind == "b":
                        p = m - ITEM_B
                        dve.wait_ge(b_z, 2 * max(p - 1, 0))
                        ins = dve.tensor_scalar(BQ[p % 2][:, :], ps, QSCALE, None, ALU.mult) if i == 0 else \
                            dve.tensor_copy(BK[p % 2][:, :], ps)
                    elif kind == "cv":
                        gi = (c0 - COL_CV) // 256
                        ins = dve.tensor_copy(CV[:, i, 4 * gi:4 * gi + 4, 0:HD], ps[:, 0:256].rearrange("p (h d) -> p h d", d=HD))
                    elif kind == "c":
                        p = m - ITEM_C
                        if p >= 2:
                            dve.wait_ge(c_s, units_of(p - 2)[-1] + 1)
                        dst = (CQ, CK)[i][p % 2][:, :]
                        if p >= 2:
                            dst, ps = dst.rearrange("p (c i) -> p c i", c=4), ps.rearrange("p (i c) -> p c i", c=4)
                        ins = dve.tensor_scalar(dst, ps, QSCALE, None, ALU.mult) if i == 0 else dve.tensor_copy(dst, ps)
                    else:
                        ins = dve.tensor_copy(GT[2 * (m - ITEM_GATE) + i][:, :], ps)
                    ins.then_inc(tile_out[tile % 2], 1)

                def a_prepare(h, k):
                    if k == 0:
                        dve.wait_ge(*taken(TILE0[2 * h] + 1))
                    if k == 1:
                        dve.wait_ge(p_ln, h + 1)
                        dve.scalar_tensor_tensor(W2[:, :, :], QF[:, :, :], 0.0, W1[:, :, :], ALU.min, ALU.subtract).then_inc(p_ls, 1)
                        dve.wait_ge(p_ls, h + 1)
                        dve.wait_ge(i_diag, max(h - 1, 0))
                        dve.tensor_tensor(AK[h % 2][:, :], W2[:, 1, :], QF[:, 1, :], ALU.subtract).then_inc(p_t, 1)
                    if k == 3:
                        dve.wait_ge(p_sg, h + 1)
                        dve.tensor_tensor(AQ[h % 2][:, :], QF[:, 0, :], W2[:, 0, :], ALU.mult).then_inc(p_q, 1)
                        dve.tensor_scalar(W1[:, 0, :], W2[:, 1, :], OML[:, h:h + 1], LBC[:, h:h + 1], ALU.mult, ALU.add).then_inc(p_f, 1)
                        dve.wait_ge(p_f, 3 * h + 1)
                        dve.tensor_scalar(W1[:, 1, :], W1[:, 0, :], TINY, 1.0 / LN_LIFT * 2, ALU.max, ALU.min).then_inc(p_f, 1)
                        dve.wait_ge(p_log, 3 * h)
                        dve.tensor_scalar(MK[:, :], W1[:, 0, :], 1.0 / LN_LIFT, None, ALU.is_lt).then_inc(p_mask, 1)
                        dve.wait_ge(p_mask, h + 1)
                        dve.tensor_scalar(W1[:, 0, :], W1[:, 0, :], 1.0 / LN_LIFT, None, ALU.max).then_inc(p_f, 1)
                    if k == 6:
                        dve.wait_ge(p_lf, 2 * h + 2)
                        dve.tensor_scalar(W1[:, 1, :], W1[:, 1, :], -math.log(LN_LIFT), None, ALU.add).then_inc(p_log, 1)
                        dve.wait_ge(p_log, 3 * h + 1)
                        dve.wait_ge(p_mask, h + 1)
                        dve.copy_predicated(AB[h % 2][:, :], MK[:, :], W1[:, 1, :]).then_inc(p_log, 1)
                        dve.wait_ge(p_log, 3 * h + 2)
                        dve.tensor_tensor_scan(AB[h % 2][:, :], const("reset"), AB[h % 2][:, :], 0.0, ALU.mult, ALU.add).then_inc(p_log, 1)

                def level_out(h, k):
                    n = A_LEVELS * h + k
                    dve.wait_ge(v_mm, n + 1)
                    dve.wait_ge(v_out, n)
                    half = P >> (k + 1)
                    dve.copy_predicated(
              AS[h % 2][:, :, :].rearrange("p c (b w) -> p c b w", w=2 * half)[:, :, :, half:],
              LM[:, k, :].rearrange("p (b r) -> p b r", r=half).unsqueeze(1).broadcast_to([P, TT, 64 // half, half]),
              PS[:, 2 + n % 2, 0:256].rearrange("p (c b r) -> p c b r", c=TT, r=half)).then_inc(v_out, 1)

                def a_head(h, k):
                    aq, ab, ak, s = AQ[h % 2], AB[h % 2], AK[h % 2], AS[h % 2]
                    if k < A_LEVELS:
                        n = A_LEVELS * h + k
                        dve.wait_ge(v_decay, n + 1)
                        dve.wait_ge(v_mm, max(n - 1, 0))
                        if n == 0:
                            dve.wait_ge(kl_set, 2)
                        dve.wait_ge(p_k, h + 1)
                        dve.wait_ge(p_q, h + 1)
                        dve.tensor_tensor(level_view(KL[n % 2][:, :], k, 0), level_view(ak[:, :], k, 0),
                                          level_view(AE[n % 2][:, :], k, 0), ALU.mult)
                        dve.tensor_tensor(
               QL[n % 2][:, :, :].rearrange("p c t -> p (c t)").rearrange("p (b r) -> p b r", r=P >> (k + 1)),
               level_view(aq[:, :], k, 1), level_view(AE[n % 2][:, :], k, 1), ALU.mult).then_inc(v_scaled, 1)
                    if k == 0:
                        dve.wait_ge(p_log, 3 * h + 3)
                        dve.wait_ge(i_turn, h)
                        b = level_view(ab[:, :], 0)
                        dve.tensor_tensor(level_view(KD[:, :], 0), b, b[:, :, P - 1:P].broadcast_to([P, TT, P]),
                                          ALU.subtract).then_inc(i_diff, 1)
                        dve.wait_ge(i_diag, h + 1)
                        dve.wait_ge(i_o, max(h - 1, 0))
                        dve.tensor_tensor(s[:, :, :], PS[:, 4, :].rearrange("p (c t) -> p c t", c=TT),
                                          ident.unsqueeze(1).broadcast_to([P, TT, P]), ALU.mult).then_inc(i_s0, 1)
                        dve.wait_ge(i_s0, h + 1)
                    if k == 1:
                        dve.wait_ge(i_eb, h + 1)
                        dve.tensor_tensor(QB[h % 2][:, :], aq[:, :], EB[:, :], ALU.mult).then_inc(i_qb, 1)
                        dve.wait_ge(i_decay, h + 1)
                        dve.tensor_tensor(KD[:, :], KD[:, :], ak[:, :], ALU.mult).then_inc(i_kd, 1)
                    if k == 6:
                        dve.wait_ge(i_u, h + 1)
                        st = ST[h % 2]
                        dve.tensor_copy(st[:, 0, :], PS[:, 6, 0:A_V]).then_inc(i_st, 1)
                        for c in (1, 2):
                            dve.wait_ge(i_st, 3 * h + c)
                            dve.scalar_tensor_tensor(st[:, c, :], st[:, c - 1, :], EB[:, (c + 1) * P - 1:(c + 1) * P],
                                                     PS[:, 6, c * A_V:(c + 1) * A_V], ALU.mult, ALU.add).then_inc(i_st, 1)
                    if 2 <= k:
                        level_out(h, k - 2)

                def a_output(h):
                    dve.wait_ge(i_o, h + 1)
                    dve.tensor_copy(OA[:, :, h * A_V:(h + 1) * A_V],
                                    PS[:, 7, 0:256].rearrange("p (c d) -> p c d", c=TT)).then_inc(i_oout, 1)

                def a_norm(k):
                    sq = ASQ[:, :, :].rearrange("p t (h d) -> p (t h) d", d=A_V)
                    oa = OA[:, :, :].rearrange("p t (h d) -> p (t h) d", d=A_V)
                    gn = GN[:, :, :].rearrange("p t (h d) -> p (t h) d", d=A_V)
                    if k == 4:
                        dve.wait_ge(i_oout, A_HEADS)
                        dve.tensor_tensor(sq, oa, oa, ALU.mult).then_inc(an, 1)
                        dve.wait_ge(an, 1)
                        dve.tensor_reduce(ARS[:, 0, :], sq, AX.X, ALU.add).then_inc(an, 1)
                        dve.wait_ge(gn_silu, 1)
                        dve.tensor_tensor(gn, gn, NGR[:, :].unsqueeze(1).broadcast_to([P, TT * A_HEADS, A_V]), ALU.mult).then_inc(an, 1)
                    if k == 6:
                        dve.wait_ge(an_r, 1)
                        dve.tensor_tensor(oa, oa, ARS[:, 2, :].unsqueeze(2).broadcast_to([P, TT * A_HEADS, A_V]), ALU.mult).then_inc(an, 1)
                        dve.wait_ge(an, 4)
                        dve.tensor_tensor(oa, oa, gn, ALU.mult).then_inc(an, 1)

                def b_softplus(h):
                    dve.wait_ge(b_ln, h + 1)
                    dve.wait_ge(b_arg, max(h - 1, 0))
                    s, z, o = 3 * (h % 2), BZ[h % 2], BS[h % 2]
                    dve.scalar_tensor_tensor(o[:, 0:512], PS[:, 2 + s, :], 0.0, z[:, 0:512], ALU.max, ALU.add)
                    dve.scalar_tensor_tensor(o[:, 512:1024], PS[:, 3 + s, :], 0.0, z[:, 512:1024], ALU.max, ALU.add)
                    dve.scalar_tensor_tensor(o[:, 1024:1280], PS[:, 4 + s, 0:256], 0.0, z[:, 1024:1280], ALU.max, ALU.add).then_inc(b_sp, 1)

                def b_output(h):
                    dve.wait_ge(b_pv, h + 1)
                    dve.tensor_copy(OB[:, :, h * HD:(h + 1) * HD],
                                    PS[:, 4 + 3 * (h % 2), 256:512].rearrange("p (c d) -> p c d", c=TT)).then_inc(b_out, 1)

                def c_unit(n):
                    if n < NU:
                        h, t0 = units[n]
                        wide = h < C_SLOTS
                        nt, keys = (2, 2 * P) if wide else (4, P)
                        dve.wait_ge(c_s, n + 1)
                        dve.wait_ge(c_p, max(n - 1, 0))
                        cs = CS[n % 2][:, :].rearrange("p (t s) -> p t s", t=nt)
                        if wide:
                            dist = const("del0")[:, t0 * 2 * P:(t0 + 2) * 2 * P].rearrange("p (t s) -> p t s", t=nt)
                        else:
                            dist = const("del1" if h < 8 else "del2").unsqueeze(1).broadcast_to([P, 4, P])
                        dve.scalar_tensor_tensor(cs, dist, slopes[h], PS[:, 2 + n % 2, :].rearrange("p (t s) -> p t s", t=nt),
                                                 ALU.mult, ALU.add).then_inc(c_bias, 1)
                        dve.wait_ge(c_bias, n + 1)
                        most = OC[:, t0:t0 + nt, h, HD + 1:HD + 2]
                        dve.tensor_reduce(most, cs, AX.X, ALU.max).then_inc(c_max, 1)
                        dve.wait_ge(c_max, n + 1)
                        dve.tensor_tensor(cs, cs, most.broadcast_to([P, nt, keys]), ALU.subtract).then_inc(c_sub, 1)
                    if n >= 2:
                        q = n - 2
                        h, t0 = units[q]
                        nt = 2 if h < C_SLOTS else 4
                        dve.wait_ge(c_pv, q + 1)
                        dve.tensor_copy(OC[:, t0:t0 + nt, h, 0:HD + 1],
                                        PS[:, 6 + q % 2, 0:nt * 65].rearrange("p (t d) -> p t d", t=nt)).then_inc(c_out, 1)

                def combine(k):
                    o = [OC[:, :, 0:4, :], OCN[:, :, 0:4, :], OCN[:, :, 4:8, :]]
                    mx = [x[:, :, :, HD + 1] for x in o]
                    w = [CW[:, i, :].rearrange("p (t h) -> p t h", t=TT) for i in range(5)]
                    if k == 0:
                        dve.wait_ge(c_perm, 256)
                        dve.tensor_tensor(w[0], mx[0], mx[1], ALU.max).then_inc(cmb, 1)
                        dve.wait_ge(cmb, 1)
                        dve.tensor_tensor(w[0], w[0], mx[2], ALU.max).then_inc(cmb, 1)
                        dve.wait_ge(cmb, 2)
                        for g in range(3):
                            dve.tensor_tensor(w[1 + g], mx[g], w[0], ALU.subtract).then_inc(cmb, 1)
                    if k == 3:
                        dve.wait_ge(cmb_e, 1)

                        def part(dst, g):
                            return dve.tensor_tensor(dst[:, :, :, :], o[g][:, :, :, 0:HD + 1],
                                                     w[1 + g].unsqueeze(3).broadcast_to([P, TT, C_SLOTS, HD + 1]), ALU.mult)

                        part(CX[0], 0)
                        part(CX[1], 1).then_inc(cmb, 1)
                        dve.wait_ge(cmb, 6)
                        dve.tensor_tensor(CX[0][:, :, :, :], CX[0][:, :, :, :], CX[1][:, :, :, :], ALU.add).then_inc(cmb, 1)
                        dve.wait_ge(cmb, 7)
                        part(CX[1], 2).then_inc(cmb_x, 1)
                        dve.wait_ge(cmb_x, 1)
                        dve.tensor_tensor(CX[0][:, :, :, :], CX[0][:, :, :, :], CX[1][:, :, :, :], ALU.add).then_inc(cmb, 1)
                        dve.wait_ge(cmb, 8)
                        dve.reciprocal(w[4], CX[0][:, :, :, HD]).then_inc(cmb, 1)
                        dve.wait_ge(cmb, 9)
                        dve.tensor_tensor(OF[:, :, :].rearrange("p t (h d) -> p t h d", d=HD), CX[0][:, :, :, 0:HD],
                                          w[4].unsqueeze(3).broadcast_to([P, TT, C_SLOTS, HD]), ALU.mult).then_inc(cmb, 1)

                def mixers(m, k):
                    if k == 0 and m:
                        take(m - 1, TILE0[m] - TILE0[m - 1] - 1)
                    if m % 2 and m < 2 * A_HEADS:
                        a_prepare(m // 2, k)
                    if MIX[m][0] in TOKEN_KINDS:
                        if k in (2, 4, 6):
                            take(m, k // 2 - 1)
                    elif k == 4:
                        take(m, 0)
                    if m % 2 == 0 and 0 < m <= 2 * A_HEADS:
                        a_head(m // 2 - 1, k)
                    if m % 2 and 3 <= m <= 2 * A_HEADS + 1:
                        if k == 0:
                            level_out((m - 3) // 2, A_LEVELS - 1)
                        if k == 3:
                            a_output((m - 3) // 2)
                    if m == ITEM_B + 1:
                        a_norm(k)
                    hb = 2 * (m - (ITEM_B + 2)) + k // 4
                    if k % 4 == 2 and 0 <= hb < B_HEADS:
                        b_softplus(hb)
                    if k % 4 == 3 and 1 <= hb <= B_HEADS:
                        b_output(hb - 1)
                    if (m, k) in UNIT_AT:
                        c_unit(UNIT_AT[(m, k)])
                    if m == ITEM_COMBINE:
                        combine(k)
                    if m >= ITEM_TURN and k % 4 == 2 and 2 * (m - ITEM_TURN) + k // 4 < KT:
                        ft = 2 * (m - ITEM_TURN) + k // 4
                        dve.wait_ge(yt_high, ft + 1)
                        dve.tensor_tensor(YL[ft][:, :], PS[:, 2 + ft % 4, :], YH[ft][:, :].bitcast(F32), ALU.subtract).then_inc(yt_low, 1)

                pre(0)
                ffn_in(0, G_FFN1)
                dve.wait_ge(ada_out, ADA_CHUNKS[0])
                columns(4 * ADA_FIRST, 72, (1, 2))
                dve.wait_ge(ada_cols, 8)
                post(0)
                pre(1)
                for m in range(NM):
                    for k in range(8):
                        mixers(m, k)
                take(NM - 1, 1)
                for j in range(KT):
                    if j % 2:
                        dve.wait_ge(*used(G_BR + j // 2))
                    else:
                        dve.wait_ge(br_done, j // 2 + 1)
                    dve.wait_ge(g_sig, 24)
                    dve.wait_ge(m_low, max(j - 1, 0))
                    for n in range(3):
                        ins = dve.tensor_tensor(MA[j % 2][:, n, :], PS[:, 3 * (j % 2) + n, :], GT[8 * n + j][:, :], ALU.mult)
                    ins.then_inc(br_mul, 1)
                    dve.wait_ge(br_mul, j + 1)
                    dve.tensor_tensor(MA[j % 2][:, 0, :], MA[j % 2][:, 0, :], MA[j % 2][:, 1, :], ALU.add).then_inc(br_add, 1)
                post(1)
                pre(2)
                ffn_in(1, G_FFN2)
                post(2)

            @block.gpsimd
            def _(pool):
                def low(g):
                    slot, n = g % 2, group_columns(g)
                    pool.wait_ge(w_high, g + 1)
                    pool.tensor_tensor(WL[slot][:, 0:n], RAW[slot][:, 0:n], WH[slot][:, 0:n].bitcast(F32),
                                       ALU.subtract).then_inc(w_low, 1)

                def low_part(m, q):
                    g = G_MIX + m
                    slot, n = g % 2, group_columns(g) // 4
                    part = slice(q * n, (q + 1) * n)
                    if q == 3:
                        pool.wait_ge(w_high, g + 1)
                    else:
                        pool.wait_ge(part_high, 3 * (m - 2) + q + 1)
                    ins = pool.tensor_tensor(WL[slot][:, part], RAW[slot][:, part], WH[slot][:, part].bitcast(F32), ALU.subtract)
                    if q == 3:
                        ins.then_inc(w_low, 1)

                def post(s):
                    for j in range(0, KT, 2):
                        pool.wait_ge(y_scaled, KT * s + j + 1)
                        pool.tensor_tensor(X[:, j, :], X[:, j, :], Y[:, j, :], ALU.add).then_inc(x_even, 1)

                def pre(s):
                    for j in range(1, KT, 2):
                        pool.wait_ge(h_high, KT * s + j + 1)
                        pool.tensor_scalar(U[:, j, :], U[:, j, :], 1.0, MOD[:, 24 * s + j:24 * s + j + 1],
                                           ALU.mult, ALU.add).then_inc(f_odd, 1)
                        pool.wait_ge(f_odd, 4 * s + j // 2 + 1)
                        pool.tensor_tensor(HL[:, j, :], U[:, j, :], HH[:, j, :].bitcast(F32), ALU.subtract).then_inc(h_low_odd, 1)

                def ffn_in(g0):
                    with pool.Fori(0, FI // 2) as i:
                        for u in range(2):
                            slot = (g0 + u) % 2
                            pool.wait_ge(w_high, i * 2 + (g0 + u + 3))
                            pool.tensor_tensor(WL[slot][:, :], RAW[slot][:, :], WH[slot][:, :].bitcast(F32),
                                               ALU.subtract).then_inc(w_low, 1)

                def row_groups(g0, n):
                    for i in range(n):
                        if g0 + i + 2 < NG:
                            low(g0 + i + 2)

                def a_diff(h, k):
                    n = A_LEVELS * h + k
                    pool.wait_ge(p_log, 3 * h + 3)
                    pool.wait_ge(v_decay, max(n - 1, 0))
                    w = P >> k
                    b = level_view(AB[h % 2][:, :], k)
                    pool.tensor_tensor(level_view(AD[n % 2][:, :], k), b,
                                       b[:, :, w // 2 - 1:w // 2].broadcast_to([P, SEQ // w, w]), ALU.subtract).then_inc(v_diff, 1)

                def a_head(h, k):
                    if k < A_LEVELS:
                        a_diff(h, k)

                def mixers(m, k):
                    if m % 2 == 0 and 0 < m <= 2 * A_HEADS:
                        a_head(m // 2 - 1, k)
                    if (m, k) == (1, 0):
                        for i in range(2):
                            pool.memset(KL[i][:, :], 0.0).then_inc(kl_set, 1)
                    hb = 2 * (m - (ITEM_B + 2)) + k // 4
                    if k % 4 == 2 and 0 <= hb < B_HEADS:
                        pool.wait_ge(b_sp, hb + 1)
                        for i in range(TT):
                            a = BS[hb % 2][:, ZCOL[i]:ZCOL[i] + P]
                            ins = pool.tensor_tensor(a, a, const("strict"), ALU.mult)
                        ins.then_inc(b_spm, 1)
                    if (m, k) == (ITEM_B + 3, 0):
                        pool.wait_ge(i_oout, A_HEADS)
                        pool.memset(CV[:, :, :, HD:HD + 1], 1.0).then_inc(c_ones, 1)

                low(0)
                low(1)
                pre(0)
                ffn_in(G_FFN1)
                row_groups(G_FO1, FO - 1)
                post(0)
                low(G_MIX + 1)
                pre(1)
                for m in range(NM):
                    for k in range(8):
                        mixers(m, k)
                        if 1 <= k <= 4 and m:
                            if m + 1 < NM:
                                low_part(m + 1, k - 1)
                            elif k == 1:
                                low(G_BR)
                low(G_BR + 1)
                for q in range(4):
                    for u in range(2):
                        j = 2 * q + u
                        ma = MA[j % 2]
                        pool.wait_ge(br_add, j + 1)
                        pool.tensor_tensor(ma[:, 0, :], ma[:, 0, :], ma[:, 2, :], ALU.add).then_inc(br_sum, 1)
                        pool.wait_ge(br_sum, j + 1)
                        pool.wait_ge(m_high, j + 1)
                        pool.tensor_tensor(HL[:, j, :], ma[:, 0, :], HH[:, j, :].bitcast(F32), ALU.subtract).then_inc(m_low, 1)
                    low(G_BR + q + 2)
                row_groups(G_WO, 3)
                post(1)
                low(G_WO + 5)
                pre(2)
                ffn_in(G_FFN2)
                row_groups(G_FO2, FO - 1)
                post(2)

        with nc.Block() as block:
            @block.gpsimd
            def _(pool):
                for sem in of_a_layer:
                    pool.sem_clear(sem)

    with nc.Block() as block:
        @block.sync
        def _(sp):
            for i in range(TT):
                sp.wait_ge(res_out, 2 * (i + 1))
                sp.dma_start(out[0, i * P:(i + 1) * P, :], XIN[:, i, :]).then_inc(stored, 16)
            sp.wait_ge(stored, 16 * TT)

        @block.tensor
        def _(pe):
            for i in range(TT):
                for half in range(2):
                    n = 2 * i + half
                    if n >= 2:
                        pe.wait_ge(res_out, n - 1)
                    for k in range(4):
                        mm = pe.transpose(PS[:, 1 + n % 2, k * P:(k + 1) * P], X[:, 4 * half + k, i * P:(i + 1) * P], ident)
                    mm.then_inc(res_turned, 1)

        @block.vector
        def _(dve):
            for n in range(2 * TT):
                dve.wait_ge(res_turned, n + 1)
                dve.tensor_copy(XIN[:, n // 2, (n % 2) * 512:(n % 2) * 512 + 512], PS[:, 1 + n % 2, :]).then_inc(res_out, 1)


_INS = ["x", "c", "w_ada", "b_ada", "norm_g", "ffn1_w_in", "ffn1_w_out", "w_in", "hgrn_lb_logits", "hgrn_norm_g",
        "w_branch_a", "w_branch_b", "w_branch_c", "w_out", "ffn2_w_in", "ffn2_w_out"]


def kernel(**inputs):
    import concourse.bacc as bacc
    from concourse.bass_utils import run_bass_kernel_spmd

    nc = bacc.Bacc("TRN2", target_bir_lowering=False, num_devices=1)
    arrays = {name: np.ascontiguousarray(inputs[name]) for name in _INS}
    arrays["const_f"], arrays["const_m"] = constants(), level_masks()
    t = {name: nc.dram_tensor(f"in_{name}", a.shape, mybir.dt.from_np(a.dtype), kind="ExternalInput").ap()
         for name, a in arrays.items()}
    out = nc.dram_tensor("out", (1, SEQ, D), F32, kind="ExternalOutput").ap()
    build(nc, t, out)
    r = run_bass_kernel_spmd(nc, [{f"in_{name}": a for name, a in arrays.items()}], core_ids=[0])
    return r.results[0]["out"]
```

```python
import math
from contextlib import ExitStack

import numpy as np

import concourse.bass as bass
from concourse import mybir

F32 = mybir.dt.float32
F32R = mybir.dt.float32r
U8 = mybir.dt.uint8
ALU = mybir.AluOpType
ACT = mybir.ActivationFunctionType
AX = mybir.AxisListType

P = 128
D = 1024
SEQ = 512
DEPTH = 2
KT = D // P
TT = SEQ // P
DFF = 2816
FT = DFF // P
EPS = 1e-6
NEG_BIG = -1e30
TINY = 1e-30

A_HEADS, A_V = 6, 64
B_HEADS, HD = 6, 64
C_HEADS, C_SLOTS = 12, 4
A_LEVELS = 7
QSCALE = HD ** -0.5
LN_LIFT = 2.0 ** 40

FI, FO = FT, FT // 2
COL_AQ, COL_AF, COL_AI, COL_AG = 0, 768, 1536, 1920
COL_BQ, COL_BK, COL_BV = 2304, 2688, 3072
COL_CQ, COL_CK, COL_CV = 3456, 4224, 4992
COL_GATE = 5760
_TOKENS = [("av", COL_AI, 256), ("av", COL_AI + 256, 128), ("ag", COL_AG, 256), ("ag", COL_AG + 256, 128),
           ("bv", COL_BV, 256), ("bv", COL_BV + 256, 128)]
MIX = ([x for h in range(A_HEADS) for x in (("a", COL_AQ + P * h, COL_AF + P * h), _TOKENS[h])]
       + [("b", COL_BQ + P * p, COL_BK + P * p) for p in range(3)]
       + [("cv", COL_CV + 256 * i, 256) for i in range(3)]
       + [("c", COL_CQ + P * p, COL_CK + P * p) for p in range(6)]
       + [("gate", COL_GATE + 256 * i, 256) for i in range(12)])
ITEM_B, ITEM_C, ITEM_GATE = 12, 18, 24
PAIR_KINDS = ("a", "b", "c")
TOKEN_KINDS = ("av", "ag", "bv", "cv")
NM = len(MIX)
G_FFN1, G_FO1 = 0, FI
G_MIX = G_FO1 + FO
G_BR = G_MIX + NM
G_WO = G_BR + 4
G_FFN2 = G_WO + 4
G_FO2 = G_FFN2 + FI
NG = G_FO2 + FO
assert NG % 2 == 0


def group_columns(g):
    if G_MIX <= g < G_BR and MIX[g - G_MIX][0] not in PAIR_KINDS:
        return KT * MIX[g - G_MIX][2]
    return 2048


TILE0 = [0]
for kind, _, _ in MIX:
    TILE0.append(TILE0[-1] + (TT if kind in TOKEN_KINDS else 2))
NTILES = TILE0[-1]
assert NTILES % 2 == 0


ROW_LASTS = (G_MIX - 1, G_FFN2 - 1, NG - 1)


def used_count(g):
    return sum(x not in ROW_LASTS for x in range(g + 1))


def loads_of(g):
    return 3 if G_BR <= g < G_WO else 2


def loads_until(g):
    return sum(loads_of(x) for x in range(g % 2, g + 1, 2))


LOADS = [loads_until(NG - 2), loads_until(NG - 1)]

ADA_ALL = 9 * D // SEQ
ADA_CHUNKS = (FI // 2, ADA_ALL - FI // 2)
ADA_FIRST = 5
ADA_OWN = ADA_ALL - ADA_FIRST - ADA_CHUNKS[0]
ADA_BEFORE = (0, ADA_CHUNKS[0])
assert 4 * ADA_FIRST >= 2 * KT and 4 * (ADA_ALL - ADA_OWN) >= 8 * KT and ADA_OWN + ADA_FIRST == ADA_CHUNKS[1] and DEPTH == 2

CONST = {}
_at = 0
for _name, _n in (("ident", P), ("ones", P), ("ntri", P), ("nones", P), ("strict", P), ("negm", P),
                  ("reset", SEQ), ("del0", TT * 2 * P), ("del1", P), ("del2", P)):
    CONST[_name] = (_at, _n)
    _at += _n
NCONST = _at


def alibi_slopes(n):
    def pow2(m):
        start = 2.0 ** (-8.0 / m)
        return [start ** (i + 1) for i in range(m)]
    c = 2 ** int(math.floor(math.log2(n)))
    s = pow2(n) if c == n else pow2(c) + pow2(2 * c)[0::2][: n - c]
    return [float(np.float32(x)) for x in sorted(s, reverse=True)]


def constants():
    t = np.zeros((P, NCONST), np.float32)
    i, j = np.arange(P)[:, None], np.arange(P)[None, :]

    def put(name, a):
        at, n = CONST[name]
        t[:, at:at + n] = np.broadcast_to(a, (P, n))

    put("ident", (i == j) * 1.0)
    put("ones", 1.0)
    put("ntri", (i >= j) * -1.0)
    put("nones", -1.0)
    put("strict", (i < j) * 1.0)
    put("negm", np.where(i < j, 0.0, NEG_BIG))
    put("reset", (np.arange(SEQ)[None, :] % P != 0) * 1.0)
    tile, key = np.arange(TT)[:, None], np.arange(2 * P)[None, :]
    delta = i[:, :, None] + P - key[None]
    valid = (delta >= 0) & (delta <= P) & (P * (tile[None] - 1) + key[None] >= 0)
    put("del0", np.where(valid, -delta, NEG_BIG).reshape(P, -1))
    put("del1", np.where(i >= j, -4.0 * (i - j), NEG_BIG))
    put("del2", np.where((i >= j) & ((i - j) % 4 == 0), -4.0 * (i - j), NEG_BIG))
    return t


def level_masks():
    m = np.zeros((P, A_LEVELS, P // 2), np.float32)
    for lev in range(A_LEVELS):
        w = P >> lev
        for t in range(P // 2):
            b = t // (w // 2)
            m[b * w:b * w + w // 2, lev, t] = 1
    return m.reshape(P, -1)


def build(nc, t, out):
    ctx = ExitStack()
    with ctx:
        body(nc, ctx, t, out)


def body(nc, ctx, t, out):
    slopes = alibi_slopes(C_HEADS)
    base = (nc.sbuf_base + 31) // 32 * 32
    at = [base]

    def sb(name, shape, dtype=F32, offset=None):
        size = int(np.prod(shape[1:])) * (1 if dtype == U8 else 4)
        if offset is None:
            offset, at[0] = at[0], at[0] + (size + 31) // 32 * 32
        assert offset + size <= nc.sbuf_usable_end, (name, offset + size, nc.sbuf_usable_end)
        return nc.alloc_sbuf_tensor_at(name, shape, dtype, offset=offset)

    X = sb("X", [P, KT, SEQ])
    HH = sb("HH", [P, KT, SEQ], F32R)
    HL = sb("HL", [P, KT, SEQ], F32R)
    RAW = [sb(f"RAW{i}", [P, 2048]) for i in range(2)]
    WH = [sb(f"WH{i}", [P, 2048], F32R) for i in range(2)]
    WL = [sb(f"WL{i}", [P, 2048], F32R) for i in range(2)]
    CT = sb("CT", [P, NCONST])
    LM = sb("LM", [P, A_LEVELS, P // 2], U8)
    CC = sb("CC", [P, KT])
    COLS = sb("COLS", [P, DEPTH, 120])
    MOD = sb("MOD", [P, 72])
    PRE = sb("PRE", [P, 3, KT])
    POST = sb("POST", [P, 3, KT])
    LB = sb("LB", [P, DEPTH, A_HEADS])
    LBW = sb("LBW", [P, 4, A_HEADS])
    LBC = sb("LBC", [P, A_HEADS])
    OML = sb("OML", [P, A_HEADS])
    EPSC = sb("EPSC", [P, 1])
    NGR = sb("NGR", [P, A_V])
    phase = at[0]

    def const(name):
        a, n = CONST[name]
        return CT[:, a:a + n]

    ident, ones = const("ident"), const("ones")

    GH = sb("GH", [P, FT, SEQ], F32R, phase)
    GL = sb("GL", [P, FT, SEQ], F32R, phase + FT * 2048)
    at[0] = phase + 2 * FT * 2048
    SB = [sb(f"SB{i}", [P, SEQ]) for i in range(2)]
    AW = [sb(f"AW{i}", [P, SEQ]) for i in range(2)]
    AACC = [sb("AACC0", [P, SEQ])]
    AWB = [sb(f"AWB{i}", [P, KT, SEQ], F32, phase + 16384 * i) for i in range(3)]
    AWT = [sb(f"AWT{i}", [P, 2, SEQ], F32, phase + 71680 + 4096 * i) for i in range(2)]
    AACC.append(sb("AACC1", [P, SEQ], F32, phase + 69632))
    Y = sb("Y", [P, KT, SEQ], F32, phase)
    NSQ = [sb(f"NSQ{i}", [P, 2, SEQ], F32, phase + 16384 + 4096 * i) for i in range(2)]
    NSS = [sb(f"NSS{i}", [P, SEQ], F32, phase + o) for i, o in enumerate((24576, 26624, 49152, 51200))]
    NLN = sb("NLN", [P, SEQ], F32, phase + 28672)
    NR = sb("NR", [P, SEQ], F32, phase + 30720)
    U = sb("U", [P, KT, SEQ], F32, phase + 32768)
    XIN = sb("XIN", [P, TT, D], F32, phase + 49152)
    ROWS = sb("ROWS", [P, P], F32, phase + 65536)
    LMF = sb("LMF", [P, A_LEVELS * P // 2], F32, phase + 66560)
    ROWL = [sb(f"ROWL{i}", [P, P], F32, phase + 68608 + 512 * i) for i in range(DEPTH)]

    OA = sb("OA", [P, TT, A_HEADS * A_V], F32, phase)
    OB = sb("OB", [P, TT, B_HEADS * HD], F32, phase + 6144)
    OF = sb("OF", [P, TT, C_SLOTS * HD], F32, phase + 12288)
    r1 = phase + 16384
    AQ = [sb(f"AQ{i}", [P, SEQ], F32, r1 + 2048 * i) for i in range(2)]
    AB = [sb(f"AB{i}", [P, SEQ], F32, r1 + 4096 + 2048 * i) for i in range(2)]
    AK = [sb(f"AK{i}", [P, SEQ], F32, r1 + 8192 + 2048 * i) for i in range(2)]
    AV = sb("AV", [P, TT, A_HEADS * A_V], F32, r1 + 12288)
    GN = sb("GN", [P, TT, A_HEADS * A_V], F32, r1 + 18432)
    QF = sb("QF", [P, 2, SEQ], F32, r1 + 24576)
    W1 = sb("W1", [P, 2, SEQ], F32, r1 + 28672)
    W2 = sb("W2", [P, 2, SEQ], F32, r1 + 32768)
    MK = sb("MK", [P, SEQ], U8, r1 + 36864)
    AD = [sb(f"AD{i}", [P, SEQ], F32, r1 + 37376 + 2048 * i) for i in range(2)]
    AE = [sb(f"AE{i}", [P, SEQ], F32, r1 + 41472 + 2048 * i) for i in range(2)]
    KL = [sb(f"KL{i}", [P, SEQ], F32, r1 + 45568 + 2048 * i) for i in range(2)]
    QL = [sb(f"QL{i}", [P, TT, P // 2], F32, r1 + 49664 + 1024 * i) for i in range(2)]
    AS = [sb(f"AS{i}", [P, TT, P], F32, r1 + 51712 + 2048 * i) for i in range(2)]
    QB = [sb(f"QB{i}", [P, SEQ], F32, r1 + 55808 + 2048 * i) for i in range(2)]
    EB = sb("EB", [P, SEQ], F32, r1 + 59904)
    KD = sb("KD", [P, SEQ], F32, r1 + 61952)
    KDT = sb("KDT", [P, TT - 1, P], F32, r1 + 64000)
    ST = [sb(f"ST{i}", [P, TT - 1, A_V], F32, r1 + 65536 + 768 * i) for i in range(2)]
    ARS = sb("ARS", [P, 3, TT * A_HEADS], F32, r1 + 67072)
    ASQ = sb("ASQ", [P, TT, A_HEADS * A_V], F32, r1 + 55808)
    BQ = [sb(f"BQ{i}", [P, SEQ], F32, r1 + 67584 + 2048 * i) for i in range(2)]
    BK = [sb(f"BK{i}", [P, SEQ], F32, r1 + 71680 + 2048 * i) for i in range(2)]
    BV = sb("BV", [P, TT, B_HEADS * HD], F32, r1 + 75776)
    BZ = [sb(f"BZ{i}", [P, 1280], F32, r1 + 24576 + 5120 * i) for i in range(2)]
    BS = [sb(f"BS{i}", [P, 1280], F32, r1 + 34816 + 5120 * i) for i in range(2)]
    BA = [sb(f"BA{i}", [P, 1280], F32, r1 + 45056 + 5120 * i) for i in range(2)]
    CV = sb("CV", [P, TT, C_HEADS, HD + 1], F32, r1)
    CQ = [sb(f"CQ{i}", [P, SEQ], F32, r1 + 12480 + 2048 * i) for i in range(2)]
    CK = [sb(f"CK{i}", [P, SEQ], F32, r1 + 16576 + 2048 * i) for i in range(2)]
    CS = [sb(f"CS{i}", [P, SEQ], F32, r1 + 24576 + 2048 * i) for i in range(2)]
    CP = [sb(f"CP{i}", [P, SEQ], F32, r1 + 28672 + 2048 * i) for i in range(2)]
    CPT = [sb(f"CPT{i}", [P, SEQ], F32, r1 + 32768 + 2048 * i) for i in range(2)]
    OC = sb("OC", [P, TT, C_HEADS, HD + 2], F32, r1 + 55296)
    OCN = sb("OCN", [P, TT, 8, HD + 2], F32, r1 + 67968)
    CW = sb("CW", [P, 5, TT * C_SLOTS], F32, r1 + 24576)
    CX = [sb(f"CX{i}", [P, TT, C_SLOTS, HD + 1], F32, r1 + 24960 + 4160 * i) for i in range(2)]
    gate_at = ([20672 + 32] + [36864 + 2048 * i for i in range(9)] + [76416 + 2048 * i for i in range(4)]
               + [24576 + 2048 * i for i in range(6)] + [67968 + 2048 * i for i in range(4)])
    GT = [sb(f"GT{i}", [P, SEQ], F32, r1 + o) for i, o in enumerate(gate_at)]
    y_at = [2048 * i for i in range(10)] + [55296 + 2048 * i for i in range(6)]
    YH = [sb(f"YH{i}", [P, SEQ], F32R, r1 + y_at[i]) for i in range(KT)]
    YL = [sb(f"YL{i}", [P, SEQ], F32R, r1 + y_at[KT + i]) for i in range(KT)]
    MA = [sb(f"MA{i}", [P, 3, SEQ], F32, phase + 6144 * i) for i in range(2)]

    PS = ctx.enter_context(nc.psum_tensor("PS", [P, 8, 512], F32))

    semaphores = []

    def sig(name, per_layer=0):
        semaphores.append(ctx.enter_context(nc.semaphore(name)))
        return semaphores[-1]

    const_in, c_rows_in, x_in = sig("const_in"), sig("c_rows_in"), sig("x_in")
    c_turned, c_out_of_psum, c_act, lb_exp = sig("c_turned"), sig("c_out_of_psum"), sig("c_act"), sig("lb_exp")
    lb_step, lb_part, eps_set, mask_set = sig("lb_step"), sig("lb_part"), sig("eps_set"), sig("mask_set")
    x_turned, x_out = sig("x_turned"), sig("x_out")
    rowl_in, cols_turned, cols_out = sig("rowl_in"), sig("cols_turned"), sig("cols_out")
    first_in, first_part, first_pair, first_sum, first_out = (
        [sig(f"first_in{i}") for i in range(3)], sig("first_part"), sig("first_pair"), sig("first_sum"), sig("first_out"))
    first_loaded, first_high = [sig(f"first_loaded{i}") for i in range(2)], sig("first_high")
    res_turned, res_out, stored = sig("res_turned"), sig("res_out"), sig("stored")

    loaded = [sig(f"loaded{i}", 16 * LOADS[i] - 32) for i in range(2)]
    w_high, w_low, w_used = sig("w_high", NG - 2), sig("w_low", NG - 2), sig("w_used", used_count(NG - 1))
    next_loaded, next_high = [sig(f"next_loaded{i}", 32) for i in range(2)], sig("next_high", 2)
    part_high = sig("part_high", 3 * (NM - 2))
    ngr_in, lb_out = sig("ngr_in", 16), sig("lb_out", 1)
    ada_in = [sig(f"ada_in{j}", 16 * 18 * KT // 2) for j in range(2)]
    ada_part, ada_sum, ada_out, ada_cols = (
        sig("ada_part", 19 * KT), sig("ada_sum", 18), sig("ada_out", 18), sig("ada_cols", 9))
    n_sq, n_ss, n_mm, n_ln, n_r = sig("n_sq", 48), sig("n_ss", 24), sig("n_mm", 24), sig("n_ln", 6), sig("n_r", 6)
    y_done, y_copied, y_scaled, x_even, x_odd = (
        sig(n, c) for n, c in (("y_done", 24), ("y_copied", 24), ("y_scaled", 24), ("x_even", 12), ("x_odd", 12)))
    u_done, h_high, f_odd, h_low_even, h_low_odd = (
        sig("u_done", 24), sig("h_high", 24), sig("f_odd", 12), sig("h_low_even", 12), sig("h_low_odd", 12))
    a_done, silu_done, gated, g_high, g_low = (sig(n, 2 * FT) for n in ("a_done", "silu_done", "gated", "g_high", "g_low"))
    tile_done = sig("tile_done", NTILES - NM)
    tile_out = [sig(f"tile_out{i}", NTILES // 2) for i in range(2)]
    p_abs, p_e, p_ln, p_ls, p_t, p_sg, p_sn, p_q, p_k = (
        sig(n, A_HEADS) for n in ("p_abs", "p_e", "p_ln", "p_ls", "p_t", "p_sg", "p_sn", "p_q", "p_k"))
    p_f, p_lf, p_log, p_mask = sig("p_f", 3 * A_HEADS), sig("p_lf", 2 * A_HEADS), sig("p_log", 3 * A_HEADS), sig("p_mask", A_HEADS)
    NL = A_HEADS * A_LEVELS
    v_diff, v_decay, v_scaled, v_mm, v_out = (sig(n, NL) for n in ("v_diff", "v_decay", "v_scaled", "v_mm", "v_out"))
    i_diag, i_s0, i_diff, i_decay, i_kd, i_eb, i_qb, i_turn, i_kdt, i_u, i_o, i_oout = (
        sig(n, A_HEADS) for n in ("i_diag", "i_s0", "i_diff", "i_decay", "i_kd", "i_eb", "i_qb", "i_turn", "i_kdt",
                                  "i_u", "i_o", "i_oout"))
    i_st, kl_set, i_qk = sig("i_st", 3 * A_HEADS), sig("kl_set", 2), sig("i_qk", A_HEADS)
    gn_silu, an, an_ln, an_r = sig("gn_silu", 1), sig("an", 5), sig("an_ln", 1), sig("an_r", 1)
    b_z, b_abs, b_e, b_ln, b_sp, b_spm, b_arg, b_a, b_pv, b_out = (
        sig(n, B_HEADS) for n in ("b_z", "b_abs", "b_e", "b_ln", "b_sp", "b_spm", "b_arg", "b_a", "b_pv", "b_out"))
    units = [(h, i) for h in range(C_HEADS) for i in ((0, 2) if h < C_SLOTS else (0,))]
    NU = len(units)
    c_s, c_bias, c_max, c_sub, c_p, c_t, c_pt, c_pv, c_out = (
        sig(n, NU) for n in ("c_s", "c_bias", "c_max", "c_sub", "c_p", "c_t", "c_pt", "c_pv", "c_out"))
    c_ones, c_perm, cmb, cmb_e = sig("c_ones", 1), sig("c_perm", 16 * 16), sig("cmb", 10), sig("cmb_e", 1)
    cmb_x = sig("cmb_x", 1)
    yt_done, yt_high, yt_low = sig("yt_done", KT), sig("yt_high", KT), sig("yt_low", KT)
    g_sig = sig("g_sig", 24)
    br_done, br_mul, br_add, m_high, m_low, br_sum = (
        sig("br_done", KT // 2), sig("br_mul", KT), sig("br_add", KT), sig("m_high", KT), sig("m_low", KT), sig("br_sum", KT))

    def units_of(pair):
        return [n for n, (h, _) in enumerate(units) if h // 2 == pair]

    UNIT_AT = {}
    for pair in range(C_HEADS // 2):
        for q, n in enumerate(units_of(pair)):
            UNIT_AT[(ITEM_C + 1 + pair, q * 8 // len(units_of(pair)))] = n
    UNIT_AT[(ITEM_C + 7, 0)], UNIT_AT[(ITEM_C + 7, 3)] = NU, NU + 1
    ITEM_COMBINE, ITEM_TURN = 27, 28

    def used(g):
        return (y_done, KT * (ROW_LASTS.index(g) + 1)) if g in ROW_LASTS else (w_used, used_count(g))

    def projected(m, i):
        return used(G_MIX + m) if i == TILE0[m + 1] - TILE0[m] - 1 else (tile_done, TILE0[m] - m + i + 1)

    def taken(tile):
        return tile_out[tile % 2], tile // 2 + 1

    def z_at(i, h):
        return {0: (2 + 3 * (h % 2), 0), 1: (3 + 3 * (h % 2), 0), 3: (3 + 3 * (h % 2), 384), 2: (4 + 3 * (h % 2), 0)}[i]

    ZCOL = {0: 0, 1: 512, 3: 896, 2: 1024}

    def zw(i):
        return SEQ - P * i

    def level_keys(lev):
        return P - (P >> (lev + 1))

    def level_view(ap, lev, half=None):
        w = P >> lev
        v = ap.rearrange("p (b w) -> p b w", w=w)
        return v if half is None else v[:, :, half * (w // 2):(half + 1) * (w // 2)]

    def first_group(w, u):
        raw = RAW[u][:, :].rearrange("p (k h c) -> p k h c", k=KT, h=2)
        w = w.rearrange("o (k p) (h c) -> p (o k) h c", p=P, h=2)
        return [(raw[:, :, h, :], w[:, :, h, u * P:(u + 1) * P]) for h in range(2)]

    def count_first_groups(pool):
        for i in range(2):
            pool.sem_inc(loaded[i], 32)
        pool.sem_inc(w_high, 2)
        pool.sem_inc(w_low, 2)

    with nc.Block() as block:
        @block.sync
        def _(sp):
            sp.dma_start(CT[:, :], t["const_f"]).then_inc(const_in, 16)
            sp.dma_start(LMF[:, :], t["const_m"]).then_inc(const_in, 16)
            sp.dma_start(ROWS[0:8, :], t["c"].rearrange("o (k p) -> (o k) p", p=P)).then_inc(c_rows_in, 16)
            sp.dma_start(ROWS[8:20, :], t["hgrn_lb_logits"].rearrange("l (k p) -> (l k) p", p=P)).then_inc(c_rows_in, 16)
            w = t["w_ada"].rearrange("l (k p) c -> p l k c", p=P)
            for ch in range(ADA_FIRST):
                if ch >= 3:
                    sp.wait_ge(first_part, (KT - 2) * (ch - 2))
                    sp.wait_ge(first_pair, ch - 2)
                sp.dma_start(AWB[ch % 3][:, :, :], w[:, 0, :, ch * SEQ:(ch + 1) * SEQ]).then_inc(first_in[ch % 3], 16)
                if ch == ADA_FIRST - 2:
                    for u in range(2):
                        for dst, src in first_group(t["ffn1_w_in"][0:1], u):
                            sp.dma_start(dst, src).then_inc(first_loaded[u], 16)
                if ch == 0:
                    for l in range(DEPTH):
                        sp.dma_start(ROWL[l][0:72, :], t["b_ada"][l].rearrange("(k p) -> k p", p=P)).then_inc(rowl_in, 16)
                        sp.dma_start(ROWL[l][72:120, :], t["norm_g"][l].rearrange("n (k p) -> (n k) p", p=P)).then_inc(
                            rowl_in, 16)
                    sp.dma_start(XIN[:, :, :], t["x"].rearrange("o (t p) d -> p (o t) d", p=P)).then_inc(x_in, 16)

        @block.tensor
        def _(pe):
            pe.wait_ge(const_in, 32)
            pe.wait_ge(c_rows_in, 32)
            pe.transpose(PS[:, 0, 0:20], ROWS[0:20, :], ident[0:20, 0:20]).then_inc(c_turned, 1)
            pe.wait_ge(rowl_in, 32 * DEPTH)
            for l in range(DEPTH):
                pe.transpose(PS[:, 3, l * P:l * P + 120], ROWL[l][0:120, :], ident[0:120, 0:120]).then_inc(cols_turned, 1)

            def chunk_sums(ch):
                if ch >= 2:
                    pe.wait_ge(first_out, ch - 1)
                pe.wait_ge(first_pair, ch + 1)
                for e, part in enumerate((AWT[ch % 2][:, 0, :], AWT[ch % 2][:, 1, :], AACC[ch % 2][:, :])):
                    if e == 2:
                        pe.wait_ge(first_part, (KT - 2) * (ch + 1))
                    for q in range(4):
                        mm = pe.matmul(PS[:, 4 + ch % 2, q:q + 1], part[:, q * P:(q + 1) * P], ones[:, 0:1],
                                       start=(e == 0 and q == 0), stop=(e == 2), skip_group_check=True)
                mm.then_inc(first_sum, 1)

            chunk_sums(0)
            pe.wait_ge(x_in, 16)
            for k in range(KT):
                if k >= 2:
                    pe.wait_ge(x_out, k - 1)
                for i in range(TT):
                    mm = pe.transpose(PS[:, 1 + k % 2, i * P:(i + 1) * P], XIN[:, i, k * P:(k + 1) * P], ident)
                mm.then_inc(x_turned, 1)
            for ch in range(1, ADA_FIRST):
                chunk_sums(ch)

        @block.scalar
        def _(act):
            act.wait_ge(c_out_of_psum, 1)
            act.activation(CC[:, :], CC[:, :], ACT.Silu).then_inc(c_act, 1)
            act.wait_ge(lb_step, 2)
            act.activation(LBW[:, 0:2, :], LBW[:, 0:2, :], ACT.Exp).then_inc(lb_exp, 1)
            act.wait_ge(c_act, 1)
            for ch in range(ADA_FIRST):
                act.wait_ge(first_in[ch % 3], 16 * (ch // 3 + 1))
                if ch >= 2:
                    act.wait_ge(first_sum, ch - 1)
                for e in range(2):
                    k = KT - 2 + e
                    ins = act.activation(AWT[ch % 2][:, e, :], AWB[ch % 3][:, k, :], ACT.Copy, scale=CC[:, k:k + 1])
                ins.then_inc(first_pair, 1)
                u = ch - (ADA_FIRST - 2)
                if u >= 0:
                    act.wait_ge(first_loaded[u], 32)
                    act.activation(WH[u][:, :], RAW[u][:, :], ACT.Copy).then_inc(first_high, 1)

        @block.gpsimd
        def _(pool):
            for u in range(2):
                pool.wait_ge(first_high, u + 1)
                pool.tensor_tensor(WL[u][:, :], RAW[u][:, :], WH[u][:, :].bitcast(F32), ALU.subtract)
            count_first_groups(pool)

        @block.vector
        def _(dve):
            dve.memset(EPSC[:, :], EPS).then_inc(eps_set, 1)
            dve.wait_ge(const_in, 32)
            dve.tensor_scalar(LM[:, :, :], LMF[:, :].rearrange("p (v r) -> p v r", v=A_LEVELS),
                              0.0, None, ALU.is_gt).then_inc(mask_set, 1)
            dve.memset(LB[:, :, :], 0.0).then_inc(lb_step, 1)
            dve.wait_ge(c_turned, 1)
            dve.tensor_copy(CC[:, :], PS[:, 0, 0:8])
            dve.tensor_copy(LBW[:, 0:2, :], PS[:, 0, 8:20].rearrange("p (l h) -> p l h", l=2)).then_inc(c_out_of_psum, 1)
            dve.wait_ge(c_out_of_psum, 1)
            dve.tensor_tensor(LBW[:, 2, :], LBW[:, 0, :], LBW[:, 1, :], ALU.max).then_inc(lb_part, 1)
            dve.wait_ge(lb_part, 1)
            dve.tensor_tensor(LBW[:, 0:2, :], LBW[:, 0:2, :],
                              LBW[:, 2:3, :].broadcast_to([P, 2, A_HEADS]), ALU.subtract).then_inc(lb_step, 1)

            def chunk(ch):
                for k in range(KT - 2):
                    acc, w = AACC[ch % 2][:, :], AWB[ch % 3][:, k, :]
                    if k == 0:
                        dve.wait_ge(first_in[ch % 3], 16 * (ch // 3 + 1))
                        ins = dve.tensor_scalar(acc, w, CC[:, k:k + 1], None, ALU.mult)
                    else:
                        dve.wait_ge(first_part, (KT - 2) * ch + k)
                        ins = dve.scalar_tensor_tensor(acc, w, CC[:, k:k + 1], acc, ALU.mult, ALU.add)
                    ins.then_inc(first_part, 1)

            dve.wait_ge(c_act, 1)
            chunk(0)
            for k in range(KT):
                dve.wait_ge(x_turned, k + 1)
                dve.tensor_copy(X[:, k, :], PS[:, 1 + k % 2, :]).then_inc(x_out, 1)
                if k == 1:
                    dve.wait_ge(lb_exp, 1)
                    dve.tensor_tensor(LBW[:, 2, :], LBW[:, 0, :], LBW[:, 1, :], ALU.add).then_inc(lb_part, 1)
                    dve.wait_ge(lb_part, 2)
                    dve.reciprocal(LBW[:, 3, :], LBW[:, 2, :]).then_inc(lb_part, 1)
                    dve.wait_ge(lb_part, 3)
                    dve.tensor_tensor(LB[:, 1, :], LBW[:, 1, :], LBW[:, 3, :], ALU.mult).then_inc(lb_part, 1)
            dve.wait_ge(cols_turned, DEPTH)
            for l in range(DEPTH):
                dve.tensor_copy(COLS[:, l, :], PS[:, 3, l * P:l * P + 120]).then_inc(cols_out, 1)
            for ch in range(1, ADA_FIRST + 1):
                if ch < ADA_FIRST:
                    chunk(ch)
                dve.wait_ge(first_sum, ch)
                dve.tensor_copy(MOD[:, 4 * ch - 4:4 * ch], PS[:, 5 - ch % 2, 0:4]).then_inc(first_out, 1)

    with nc.Fori(0, DEPTH) as l:
        with nc.Block() as block:
            @block.sync
            def _(sp):
                def of_layer(name):
                    return t[name][bass.ds(l, 1)]

                sp.dma_start(NGR[:, :], of_layer("hgrn_norm_g").broadcast_to([P, A_V])).then_inc(ngr_in, 16)
                def load(g, pieces):
                    sp.wait_ge(w_low, max(g - 1, 0))
                    for dst, src in pieces:
                        sp.dma_start(dst, src).then_inc(loaded[g % 2], 16)

                def ffn(f, g0, name, g1, name_out):
                    w = of_layer(name).rearrange("o (k p) (h c) -> p (o k) h c", p=P, h=2)
                    own, other = (t["w_ada"][bass.ds(x, 1)].rearrange("o (k p) c -> p (o k) c", p=P)
                                  for x in (l, l * -1 + (DEPTH - 1)))

                    def raw(u):
                        return RAW[(g0 + u) % 2][:, :].rearrange("p (k h c) -> p k h c", k=KT, h=2)

                    def pieces(i, u, w_ada, ch0):
                        for k in range(4 * u, 4 * u + 4):
                            sp.wait_ge(ada_part, i * KT + ((ADA_BEFORE[f] + 1) * KT + k - 1))
                            columns = w_ada[:, k, bass.ds(i * SEQ + ch0 * SEQ, SEQ)]
                            sp.dma_start(AW[k % 2][:, :], columns).then_inc(ada_in[k % 2], 16)

                    for u in range(2 if f else 0):
                        load(g0 + u, [(raw(u)[:, :, h, :], w[:, :, h, u * P:(u + 1) * P]) for h in range(2)])

                    def next_group(i, u):
                        sp.wait_ge(w_low, i * 2 + (g0 + u + 1))
                        for h in range(2):
                            sp.dma_start(raw(u)[:, :, h, :], w[:, :, h, bass.ds(i * 2 * P + (u + 2) * P, P)]).then_inc(
                                loaded[(g0 + u) % 2], 16)

                    last = FI // 2 - 1
                    if f == 0:
                        with sp.Fori(0, last) as i:
                            for u in range(2):
                                pieces(i, u, own, ADA_FIRST)
                                next_group(i, u)
                        for u in range(2):
                            row_groups(g1, name_out, u, u + 1)
                            pieces(last, u, own, ADA_FIRST)
                    else:
                        with sp.Fori(0, ADA_OWN) as i:
                            for u in range(2):
                                pieces(i, u, own, ADA_ALL - ADA_OWN)
                                next_group(i, u)
                        with sp.Fori(ADA_OWN, ADA_CHUNKS[1]) as i:
                            for u in range(2):
                                pieces(i, u, other, -ADA_OWN)
                                next_group(i, u)
                        with sp.Fori(ADA_CHUNKS[1], last) as i:
                            for u in range(2):
                                next_group(i, u)
                        row_groups(g1, name_out, 0, 2)
                    row_groups(g1, name_out, 2, FO)

                def row_groups(g0, name, i0, i1):
                    w = of_layer(name).rearrange("o (g k p) c -> p (o g) k c", p=P, k=2)
                    for i in range(i0, i1):
                        raw = RAW[(g0 + i) % 2][:, :].rearrange("p (k c) -> p k c", k=2)
                        load(g0 + i, [(raw[:, k, :], w[:, i, k, :]) for k in range(2)])

                ffn(0, G_FFN1, "ffn1_w_in", G_FO1, "ffn1_w_out")
                w = of_layer("w_in").rearrange("o (k p) c -> p (o k) c", p=P)
                for m, (kind, c0, c1) in enumerate(MIX):
                    raw = RAW[(G_MIX + m) % 2]
                    if kind in PAIR_KINDS:
                        v = raw[:, :].rearrange("p (k h c) -> p k h c", k=KT, h=2)
                        load(G_MIX + m, [(v[:, :, h, :], w[:, :, c:c + P]) for h, c in enumerate((c0, c1))])
                    else:
                        v = raw[:, 0:KT * c1].rearrange("p (k c) -> p k c", k=KT)
                        load(G_MIX + m, [(v[:, k:k + 4, :], w[:, k:k + 4, c0:c0 + c1]) for k in (0, 4)])
                for i in range(4):
                    raw = RAW[(G_BR + i) % 2][:, :].rearrange("p (k c) -> p k c", k=KT)
                    load(G_BR + i, [(raw[:, k0:k0 + n, :],
                                     of_layer(name).rearrange("o (k p) c -> p (o k) c", p=P)[:, :, 256 * i:256 * i + 256])
                                    for name, k0, n in (("w_branch_a", 0, 3), ("w_branch_b", 3, 3), ("w_branch_c", 6, 2))])
                row_groups(G_WO, "w_out", 0, 4)
                ffn(1, G_FFN2, "ffn2_w_in", G_FO2, "ffn2_w_out")
                for u in range(2):
                    sp.wait_ge(w_low, NG - 1 + u)
                    for dst, src in first_group(t["ffn1_w_in"][bass.ds(l * -1 + (DEPTH - 1), 1)], u):
                        sp.dma_start(dst, src).then_inc(next_loaded[u], 16)

            @block.tensor
            def _(pe):
                def three(o, ah, al, bh, bl, start, stop):
                    pe.matmul(o, ah, bh, start=start, stop=False)
                    pe.matmul(o, ah, bl, start=False, stop=False)
                    return pe.matmul(o, al, bh, start=False, stop=stop)

                def norm_sum(n, q):
                    pe.wait_ge(n_ss, 4 * n + q + 1)
                    pe.matmul(PS[:, 1 - n % 2, :], ones, NSS[q][:, :], start=(q == 0), stop=(q == 3)).then_inc(n_mm, 1)

                def input_tile(s, k):
                    pe.wait_ge((h_low_even, h_low_odd)[k % 2], 4 * s + k // 2 + 1)

                def ffn_in(s, f, g0):
                    def group(u):
                        wh = WH[(g0 + u) % 2][:, :].rearrange("p (k h c) -> p k h c", k=KT, h=2)
                        wl = WL[(g0 + u) % 2][:, :].rearrange("p (k h c) -> p k h c", k=KT, h=2)
                        for half in range(2):
                            for k in range(KT):
                                mm = three(PS[:, 2 * u + half, :], wh[:, k, half, :], wl[:, k, half, :],
                                           HH[:, k, :], HL[:, k, :], k == 0, k == KT - 1)
                            mm.then_inc((a_done, w_used)[half], 1)

                    if f:
                        pe.wait_ge(w_low, g0 + 2)
                    w4 = [[w[(g0 + u) % 2][:, :].rearrange("p (k h c) -> p k h c", k=KT, h=2) for w in (WH, WL)]
                          for u in range(2)]
                    order = [(k, u, half) for k in range(KT // 2) for u in range(2) for half in range(2)]
                    order += [(k, u, half) for u in range(2) for half in range(2) for k in range(KT // 2, KT)]
                    for n, (k, u, half) in enumerate(order):
                        if (u, half) == (0, 0):
                            input_tile(s, k)
                        mm = three(PS[:, 2 * u + half, :], w4[u][0][:, k, half, :], w4[u][1][:, k, half, :],
                                   HH[:, k, :], HL[:, k, :], k == 0, k == KT - 1)
                        if k == KT - 1:
                            mm.then_inc((a_done, w_used)[half], 1)

                    def ada(i):
                        pe.wait_ge(ada_part, i * KT + (ADA_BEFORE[f] + 2) * KT)
                        for q in range(4):
                            mm = pe.matmul(PS[:, 4, q:q + 1], AACC[0][:, q * P:(q + 1) * P], ones[:, 0:1],
                                           start=True, stop=True)
                        mm.then_inc(ada_sum, 1)

                    ada(0)
                    for first, end in ((1, ADA_CHUNKS[f]), (ADA_CHUNKS[f], FI // 2)):
                        if first < end:
                            with pe.Fori(first, end) as i:
                                for u in range(2):
                                    pe.wait_ge(w_low, i * 2 + (g0 + u + 1))
                                    pe.wait_ge(gated, i * 2 + (FT * f + u - 1))
                                    group(u)
                                if end == ADA_CHUNKS[f]:
                                    ada(i)

                def rows_product(g0, n, rh, rl, ready, s, bank_free=None):
                    for i in range(n):
                        pe.wait_ge(w_low, g0 + i + 1)
                        ready(i)
                        wh = WH[(g0 + i) % 2][:, :].rearrange("p (k c) -> p k c", k=2)
                        wl = WL[(g0 + i) % 2][:, :].rearrange("p (k c) -> p k c", k=2)
                        for j in range(KT):
                            if i == 0 and bank_free:
                                bank_free(j)
                            for k in range(2):
                                mm = three(PS[:, j, :], wh[:, k, j * P:(j + 1) * P], wl[:, k, j * P:(j + 1) * P],
                                           rh(2 * i + k), rl(2 * i + k), i == 0 and k == 0, i == n - 1 and k == 1)
                            if i == n - 1:
                                mm.then_inc(y_done, 1)
                                if j in (3, 5, 7):
                                    norm_sum(2 * s + 1, (j - 3) // 2)
                            elif j == KT - 1:
                                mm.then_inc(w_used, 1)

                def ffn_out(s, f, g0):
                    def ready(i):
                        pe.wait_ge(g_low, FT * f + 2 * i + 2)

                    def bank_free(j):
                        if j in (0, 2):
                            pe.wait_ge(gated, FT * (f + 1) - (j == 0))
                        if j == 4:
                            pe.wait_ge(ada_out, (ADA_CHUNKS[0], ADA_ALL)[f])
                    rows_product(g0, FO, lambda k: GH[:, k, :], lambda k: GL[:, k, :], ready, s, bank_free)

                def project(m, k):
                    kind, c0, c1 = MIX[m]
                    slot = (G_MIX + m) % 2
                    if k == 0:
                        pe.wait_ge(w_low, G_MIX + m + 1)
                    if m == 0:
                        wh, wl = (w[slot][:, :].rearrange("p (k h c) -> p k h c", k=KT, h=2) for w in (WH, WL))
                        input_tile(1, k)
                        for i in range(2):
                            mm = three(PS[:, i, :], wh[:, k, i, :], wl[:, k, i, :], HH[:, k, :], HL[:, k, :], k == 0, k == 7)
                            if k == 7:
                                mm.then_inc((tile_done, w_used)[i], 1)
                        return
                    if kind in TOKEN_KINDS:
                        i, k0, nk, width = k // 2, 4 * (k % 2), 4, c1
                        wh = WH[slot][:, 0:KT * width].rearrange("p (k c) -> p k c", k=KT)
                        wl = WL[slot][:, 0:KT * width].rearrange("p (k c) -> p k c", k=KT)
                    else:
                        i, k0, nk, width = k // 4, 2 * (k % 4), 2, SEQ
                        wh = WH[slot][:, :].rearrange("p (k h c) -> p k h c", k=KT, h=2)
                        wl = WL[slot][:, :].rearrange("p (k h c) -> p k h c", k=KT, h=2)
                    tile = TILE0[m] + i
                    if k0 == 0:
                        pe.wait_ge(tile_out[tile % 2], tile // 2)
                    o = PS[:, tile % 2, 0:width]
                    for kk in range(k0, k0 + nk):
                        if kind in TOKEN_KINDS:
                            tok = slice(i, SEQ, 4) if kind == "cv" and c0 > COL_CV else slice(i * P, (i + 1) * P)
                            mm = three(o, HH[:, kk, tok], HL[:, kk, tok], wh[:, kk, :], wl[:, kk, :], kk == 0, kk == KT - 1)
                        else:
                            mm = three(o, wh[:, kk, i, :], wl[:, kk, i, :], HH[:, kk, :], HL[:, kk, :], kk == 0, kk == KT - 1)
                    if k0 + nk == KT:
                        mm.then_inc(w_used if k == 7 else tile_done, 1)

                def a_head(h, k):
                    ab = AB[h % 2]
                    if k == 0:
                        pe.wait_ge(i_qk, h + 1)
                        pe.wait_ge(i_s0, h)
                        pe.matmul(PS[:, 4, :], ones, QB[h % 2][:, :], start=True, stop=True).then_inc(i_diag, 1)
                    if k:
                        n = A_LEVELS * h + k - 1
                        keys = level_keys(k - 1)
                        pe.wait_ge(v_scaled, n + 1)
                        pe.wait_ge(v_out, max(n - 1, 0))
                        for c in range(TT):
                            mm = pe.matmul(PS[0:keys, 2 + n % 2, c * 64:(c + 1) * 64], KL[n % 2][:, c * P:c * P + keys],
                                           QL[n % 2][:, c, :], start=True, stop=True)
                        mm.then_inc(v_mm, 1)
                    if k == 3:
                        pe.wait_ge(i_kd, h + 1)
                        pe.wait_ge(i_kdt, h)
                        for c in range(TT - 1):
                            mm = pe.transpose(PS[:, 5, c * P:(c + 1) * P], KD[:, c * P:(c + 1) * P], ident)
                        mm.then_inc(i_turn, 1)
                    if k == 5:
                        pe.wait_ge(i_kdt, h + 1)
                        pe.wait_ge(i_st, 3 * h)
                        for c in range(TT - 1):
                            mm = pe.matmul(PS[:, 6, c * A_V:(c + 1) * A_V], KDT[:, c, :], AV[:, c, h * A_V:(h + 1) * A_V],
                                           start=True, stop=True)
                        mm.then_inc(i_u, 1)

                def a_output(h):
                    pe.wait_ge(v_out, A_LEVELS * (h + 1))
                    pe.wait_ge(i_qb, h + 1)
                    pe.wait_ge(i_st, 3 * h + 3)
                    pe.wait_ge(i_oout, h)
                    for c in range(TT):
                        o = PS[:, 7, c * A_V:(c + 1) * A_V]
                        mm = pe.matmul(o, AS[h % 2][:, c, :], AV[:, c, h * A_V:(h + 1) * A_V], start=True, stop=(c == 0))
                        if c:
                            mm = pe.matmul(o, QB[h % 2][:, c * P:(c + 1) * P], ST[h % 2][:, c - 1, :], start=False, stop=True)
                    mm.then_inc(i_o, 1)

                def b_scores(h):
                    pr = slice((h % 2) * HD, (h % 2) * HD + HD)
                    pe.wait_ge(*taken(TILE0[ITEM_B + h // 2] + 1))
                    if h == 0:
                        pe.wait_ge(i_oout, A_HEADS)
                    pe.wait_ge(b_out, max(h - 1, 0))
                    for i in (0, 1, 3, 2):
                        bank, col = z_at(i, h)
                        mm = pe.matmul(PS[:, bank, col:col + zw(i)], BK[h // 2 % 2][pr, i * P:(i + 1) * P],
                                       BQ[h // 2 % 2][pr, i * P:SEQ], start=(i != 3), stop=True, skip_group_check=True)
                    mm.then_inc(b_z, 1)

                def b_args(h):
                    pe.wait_ge(b_spm, h + 1)
                    for i in range(TT):
                        bank, col = z_at(i, h)
                        mm = pe.matmul(PS[:, bank, col:col + P], ident, const("negm"), start=False, stop=True, skip_group_check=True)
                        mm = pe.matmul(PS[:, bank, col:col + zw(i)], const("ntri"), BS[h % 2][:, ZCOL[i]:ZCOL[i] + zw(i)],
                                       start=False, stop=True, skip_group_check=True)
                        for j in range(i + 1, TT):
                            mm = pe.matmul(PS[:, bank, col + P * (j - i):col + zw(i)], const("nones"),
                                           BS[h % 2][:, ZCOL[j]:ZCOL[j] + zw(j)], start=False, stop=True, skip_group_check=True)
                    mm.then_inc(b_arg, 1)

                def b_values(h):
                    pe.wait_ge(b_a, h + 1)
                    for j in range(TT):
                        for i in range(j + 1):
                            a = ZCOL[i] + P * (j - i)
                            mm = pe.matmul(PS[:, 4 + 3 * (h % 2), 256 + j * HD:256 + (j + 1) * HD], BA[h % 2][:, a:a + P],
                                           BV[:, i, h * HD:(h + 1) * HD], start=(i == 0 and j == 0), stop=True,
                                           skip_group_check=True)
                    mm.then_inc(b_pv, 1)

                def c_scores(n):
                    h, t0 = units[n]
                    pair, pr = h // 2, slice((h % 2) * HD, (h % 2) * HD + HD)
                    pe.wait_ge(*taken(TILE0[ITEM_C + pair] + 1))
                    if n == 0:
                        pe.wait_ge(b_out, B_HEADS)
                    pe.wait_ge(c_bias, max(n - 1, 0))
                    for q in range(4):
                        tq, tk = (t0 + q // 2, max(t0 + q // 2 - 1 + q % 2, 0)) if h < C_SLOTS else (q, q)
                        mm = pe.matmul(PS[:, 2 + n % 2, q * P:(q + 1) * P], CQ[pair % 2][pr, tq * P:(tq + 1) * P],
                                       CK[pair % 2][pr, tk * P:(tk + 1) * P], start=True, stop=True)
                    mm.then_inc(c_s, 1)

                def c_turn(n):
                    pe.wait_ge(c_p, n + 1)
                    pe.wait_ge(c_pt, max(n - 1, 0))
                    for q in range(4):
                        mm = pe.transpose(PS[:, 4 + n % 2, q * P:(q + 1) * P], CP[n % 2][:, q * P:(q + 1) * P], ident)
                    mm.then_inc(c_t, 1)

                def c_values(n):
                    h, t0 = units[n]
                    if n == 0:
                        pe.wait_ge(*taken(TILE0[ITEM_C] - 1))
                        pe.wait_ge(*taken(TILE0[ITEM_C] - 2))
                        pe.wait_ge(c_ones, 1)
                    pe.wait_ge(c_pt, n + 1)
                    pe.wait_ge(c_out, max(n - 1, 0))
                    for q in range(4):
                        first, last = (q % 2 == 0, q % 2 == 1) if h < C_SLOTS else (True, True)
                        o, tk = (q // 2, max(t0 + q // 2 - 1 + q % 2, 0)) if h < C_SLOTS else (q, q)
                        mm = pe.matmul(PS[:, 6 + n % 2, o * 65:(o + 1) * 65], CPT[n % 2][:, q * P:(q + 1) * P], CV[:, tk, h, :],
                                       start=first, stop=last)
                    mm.then_inc(c_pv, 1)

                def turn_mixed(ft):
                    if ft == 0:
                        pe.wait_ge(an, 5)
                        pe.wait_ge(b_out, B_HEADS)
                        pe.wait_ge(cmb, 10)
                    pe.wait_ge(yt_low, max(ft - 3, 0))
                    src, c = (OA, ft) if ft < 3 else (OB, ft - 3) if ft < 6 else (OF, ft - 6)
                    for i in range(TT):
                        mm = pe.transpose(PS[:, 2 + ft % 4, i * P:(i + 1) * P], src[:, i, c * P:(c + 1) * P], ident)
                    mm.then_inc(yt_done, 1)

                def mixers(m, k):
                    if m % 2 == 0 and 0 < m <= 2 * A_HEADS:
                        a_head(m // 2 - 1, k)
                    if m % 2 and 3 <= m <= 2 * A_HEADS + 1 and k == 2:
                        a_output((m - 3) // 2)
                    hb = 2 * (m - (ITEM_B + 2)) + k // 4
                    if k % 4 == 0 and 0 <= hb < B_HEADS:
                        b_scores(hb)
                    if k % 4 == 1 and 1 <= hb <= B_HEADS:
                        b_args(hb - 1)
                    if k % 4 == 3 and 1 <= hb <= B_HEADS:
                        b_values(hb - 1)
                    if (m, k) in UNIT_AT:
                        n = UNIT_AT[(m, k)]
                        if n < NU:
                            c_scores(n)
                        if 1 <= n <= NU:
                            c_turn(n - 1)
                        if 2 <= n:
                            c_values(n - 2)
                    if m >= ITEM_TURN and k % 4 == 0 and 2 * (m - ITEM_TURN) + k // 4 < KT:
                        turn_mixed(2 * (m - ITEM_TURN) + k // 4)

                def merge():
                    pe.wait_ge(yt_low, KT)
                    pe.wait_ge(*taken(NTILES - 1))
                    pe.wait_ge(*taken(NTILES - 2))
                    for q in range(4):
                        pe.wait_ge(w_low, G_BR + q + 1)
                        wh = WH[(G_BR + q) % 2][:, :].rearrange("p (k c) -> p k c", k=KT)
                        wl = WL[(G_BR + q) % 2][:, :].rearrange("p (k c) -> p k c", k=KT)
                        for u in range(2):
                            j = 2 * q + u
                            pe.wait_ge(br_mul, max(j - 1, 0))
                            for n, (k0, k1) in enumerate(((0, 3), (3, 6), (6, 8))):
                                for k in range(k0, k1):
                                    mm = three(PS[:, 3 * (j % 2) + n, :], wh[:, k, u * P:(u + 1) * P], wl[:, k, u * P:(u + 1) * P],
                                               YH[k][:, :], YL[k][:, :], k == k0, k == k1 - 1)
                            mm.then_inc((br_done, w_used)[u], 1)

                def norms(s):
                    norm_sum(2 * s + 1, 3)
                    if s < 2:
                        for q in range(4):
                            norm_sum(2 * s + 2, q)

                for q in range(4):
                    norm_sum(0, q)
                ffn_in(0, 0, G_FFN1)
                ffn_out(0, 0, G_FO1)
                norms(0)
                for m in range(NM):
                    for k in range(8):
                        project(m, k)
                        mixers(m, k)
                merge()

                def merged(i):
                    if i == 0:
                        pe.wait_ge(br_mul, KT)
                    pe.wait_ge(m_low, 2 * i + 2)
                rows_product(G_WO, 4, lambda k: HH[:, k, :], lambda k: HL[:, k, :], merged, 1)
                norms(1)
                ffn_in(2, 1, G_FFN2)
                ffn_out(2, 1, G_FO2)
                norms(2)

            @block.scalar
            def _(act):
                def high(g):
                    slot = g % 2
                    act.wait_ge(loaded[slot], 16 * loads_until(g))
                    if g >= 2:
                        act.wait_ge(*used(g - 2))
                    n = group_columns(g)
                    act.activation(WH[slot][:, 0:n], RAW[slot][:, 0:n], ACT.Copy).then_inc(w_high, 1)

                def high_part(m, q):
                    g = G_MIX + m
                    slot, n = g % 2, group_columns(g) // 4
                    if q == 0:
                        act.wait_ge(loaded[slot], 16 * loads_until(g))
                        act.wait_ge(*used(g - 2))
                    act.activation(WH[slot][:, q * n:(q + 1) * n], RAW[slot][:, q * n:(q + 1) * n], ACT.Copy).then_inc(
                        w_high if q == 3 else part_high, 1)

                def norm(n, square, between=None):
                    for q in range(4):
                        act.wait_ge(n_ss, 4 * n + max(q - 1, 0))
                        square(q)
                    if between:
                        between()
                    act.wait_ge(n_mm, 4 * n + 4)
                    act.activation(NLN[:, :], PS[:, 1 - n % 2, :], ACT.Ln, bias=EPSC[:, 0:1], scale=1.0 / D).then_inc(
                        n_ln, 1)
                    act.wait_ge(n_ln, n + 1)
                    act.activation(NR[:, :], NLN[:, :], ACT.Exp, scale=-0.5).then_inc(n_r, 1)

                def post(s):
                    def square(q):
                        for i in range(2):
                            act.wait_ge(y_done, KT * s + 2 * q + i + 1)
                            act.activation(NSQ[q % 2][:, i, :], PS[:, 2 * q + i, :], ACT.Square).then_inc(n_sq, 1)
                    act.preload_act_table_set("natural_log_exp_and_others")
                    norm(2 * s + 1, square, (lambda: next_high_part(1)) if s == 2 else None)

                def pre(s):
                    def square(q):
                        for i in range(2):
                            if s:
                                act.wait_ge((x_even, x_odd)[i], 4 * (s - 1) + q + 1)
                            act.activation(NSQ[q % 2][:, i, :], X[:, 2 * q + i, :], ACT.Square).then_inc(n_sq, 1)
                    if s == 0:
                        act.preload_act_table_set("natural_log_exp_and_others")
                    norm(2 * s, square)

                def inputs(s):
                    for j in range(KT):
                        act.wait_ge(u_done, KT * s + j + 1)
                        act.activation(HH[:, j, :], U[:, j, :], ACT.Identity, bias=MOD[:, 24 * s + j:24 * s + j + 1]).then_inc(
                            h_high, 1)

                def ffn_in(f, g0):
                    act.preload_act_table(ACT.Silu)
                    with act.Fori(0, FI // 2) as i:
                        for u in range(2):
                            slot = (g0 + u) % 2
                            act.wait_ge(a_done, i * 2 + (FT * f + u + 1))
                            if u:
                                act.wait_ge(g_low, i * 2 + (FT * f + 1))
                            act.activation(SB[u][:, :], PS[:, 2 * u, :], ACT.Silu).then_inc(silu_done, 1)
                            act.wait_ge(w_used, i * 2 + used_count(g0 + u))
                            act.wait_ge(loaded[slot], i * 32 + 16 * loads_until(g0 + u + 2))
                            act.activation(WH[slot][:, :], RAW[slot][:, :], ACT.Copy).then_inc(w_high, 1)
                            act.wait_ge(gated, i * 2 + (FT * f + u + 1))
                            act.activation(GH[:, bass.ds(i * 2 + u, 1), :].rearrange("p o c -> p (o c)"),
                                           SB[u][:, :], ACT.Copy).then_inc(g_high, 1)

                def row_groups(g0, n):
                    for i in range(n):
                        if g0 + i + 2 < NG:
                            high(g0 + i + 2)

                def a_prepare(h, k):
                    if k == 0:
                        act.wait_ge(*taken(TILE0[2 * h]))
                        act.wait_ge(*taken(TILE0[2 * h] + 1))
                        act.wait_ge(p_mask, h)
                        act.wait_ge(p_log, 3 * h)
                        act.activation(W1[:, :, :], QF[:, :, :], ACT.Abs).then_inc(p_abs, 1)
                        act.wait_ge(p_abs, h + 1)
                        act.activation(W1[:, :, :], W1[:, :, :], ACT.Exp, scale=-1.0).then_inc(p_e, 1)
                        act.wait_ge(p_e, h + 1)
                        act.activation(W1[:, :, :], W1[:, :, :], ACT.Ln, bias=1.0).then_inc(p_ln, 1)
                    if k == 2:
                        act.wait_ge(p_t, h + 1)
                        act.activation(W2[:, :, :], W2[:, :, :], ACT.Exp).then_inc(p_sg, 1)
                        act.activation(AK[h % 2][:, :], AK[h % 2][:, :], ACT.Exp).then_inc(p_sn, 1)
                    if k == 3:
                        act.wait_ge(p_sn, h + 1)
                        act.activation(AK[h % 2][:, :], AK[h % 2][:, :], ACT.Copy, scale=OML[:, h:h + 1]).then_inc(p_k, 1)
                    if k == 5:
                        act.wait_ge(p_f, 3 * h + 3)
                        act.wait_ge(v_diff, A_LEVELS * max(h - 1, 0))
                        act.wait_ge(i_diff, max(h - 1, 0))
                        act.activation(AB[h % 2][:, :], W1[:, 0, :], ACT.Ln).then_inc(p_lf, 1)
                        act.activation(W1[:, 1, :], W1[:, 1, :], ACT.Ln, scale=LN_LIFT).then_inc(p_lf, 1)

                def a_head(h, k):
                    if k == 0:
                        act.wait_ge(p_log, 3 * h + 3)
                        act.wait_ge(i_qb, h)
                        act.wait_ge(i_st, 3 * h)
                        act.activation(EB[:, :], AB[h % 2][:, :], ACT.Exp).then_inc(i_eb, 1)
                    if k == 4:
                        act.wait_ge(i_turn, h + 1)
                        act.activation(KDT[:, :, :], PS[:, 5, 0:384].rearrange("p (c t) -> p c t", c=3), ACT.Copy).then_inc(
                            i_kdt, 1)
                    if k == 1:
                        act.wait_ge(i_diff, h + 1)
                        act.activation(KD[:, :], KD[:, :], ACT.Exp, scale=-1.0).then_inc(i_decay, 1)
                    if k < A_LEVELS:
                        n = A_LEVELS * h + k
                        act.wait_ge(v_diff, n + 1)
                        act.wait_ge(v_scaled, max(n - 1, 0))
                        act.activation(level_view(AE[n % 2][:, :], k, 0), level_view(AD[n % 2][:, :], k, 0), ACT.Exp, scale=-1.0)
                        act.activation(level_view(AE[n % 2][:, :], k, 1), level_view(AD[n % 2][:, :], k, 1), ACT.Exp).then_inc(
                            v_decay, 1)

                def take_a(m, i):
                    tile = TILE0[m] + i
                    act.wait_ge(*projected(m, i))
                    act.wait_ge((p_q, p_t)[i], m // 2)
                    act.activation(QF[:, i, :], PS[:, tile % 2, :], ACT.Copy).then_inc(tile_out[tile % 2], 1)

                def a_norm():
                    act.wait_ge(an, 2)
                    act.activation(ARS[:, 1, :], ARS[:, 0, :], ACT.Ln, bias=EPSC[:, 0:1], scale=1.0 / A_V).then_inc(
                        an_ln, 1)
                    act.wait_ge(an_ln, 1)
                    act.activation(ARS[:, 2, :], ARS[:, 1, :], ACT.Exp, scale=-0.5).then_inc(an_r, 1)

                def gates_silu():
                    act.wait_ge(*taken(TILE0[8] - 1))
                    act.wait_ge(*taken(TILE0[8] - 2))
                    act.activation(GN[:, :, :], GN[:, :, :], ACT.Silu).then_inc(gn_silu, 1)
                    act.preload_act_table_set("natural_log_exp_and_others")

                def b_softplus(h):
                    act.wait_ge(b_z, h + 1)
                    act.wait_ge(b_sp, max(h - 1, 0))
                    s = 3 * (h % 2)
                    z = BZ[h % 2]
                    act.activation(z[:, 0:512], PS[:, 2 + s, :], ACT.Abs)
                    act.activation(z[:, 512:1024], PS[:, 3 + s, :], ACT.Abs)
                    act.activation(z[:, 1024:1280], PS[:, 4 + s, 0:256], ACT.Abs).then_inc(b_abs, 1)
                    act.wait_ge(b_abs, h + 1)
                    act.activation(z[:, :], z[:, :], ACT.Exp, scale=-1.0).then_inc(b_e, 1)
                    act.wait_ge(b_e, h + 1)
                    act.activation(z[:, :], z[:, :], ACT.Ln, bias=1.0).then_inc(b_ln, 1)

                def b_weights(h):
                    act.wait_ge(b_arg, h + 1)
                    act.wait_ge(b_pv, max(h - 1, 0))
                    s = 3 * (h % 2)
                    a = BA[h % 2]
                    act.activation(a[:, 0:512], PS[:, 2 + s, :], ACT.Exp)
                    act.activation(a[:, 512:1024], PS[:, 3 + s, :], ACT.Exp)
                    act.activation(a[:, 1024:1280], PS[:, 4 + s, 0:256], ACT.Exp).then_inc(b_a, 1)

                def c_unit(n):
                    if n < NU:
                        act.wait_ge(c_sub, n + 1)
                        act.wait_ge(c_t, max(n - 1, 0))
                        act.activation(CP[n % 2][:, :], CS[n % 2][:, :], ACT.Exp).then_inc(c_p, 1)
                    if 1 <= n <= NU:
                        act.wait_ge(c_t, n)
                        act.wait_ge(c_pv, max(n - 2, 0))
                        act.activation(CPT[(n - 1) % 2][:, :], PS[:, 4 + (n - 1) % 2, :], ACT.Copy).then_inc(c_pt, 1)

                def to_token_order():
                    act.wait_ge(c_out, NU)
                    for c in range(4):
                        for j in range(TT):
                            act.dma_start(OCN[c:P:4, j, :, :], OC[32 * j:32 * j + 32, c, 4:12, :]).then_inc(c_perm, 16)

                def mixers(m, k):
                    if k == 0 and m and MIX[m - 1][0] == "a":
                        if m == 1:
                            take_a(m - 1, 0)
                        take_a(m - 1, 1)
                    if k == 4 and m and MIX[m][0] == "a":
                        take_a(m, 0)
                    if m % 2 == 0 and 0 < m <= 2 * A_HEADS:
                        a_head(m // 2 - 1, k)
                    if m % 2 and m < 2 * A_HEADS:
                        a_prepare(m // 2, k)
                    if (m, k) == (ITEM_B + 1, 0):
                        gates_silu()
                    if (m, k) == (ITEM_B + 1, 5):
                        a_norm()
                    hb = 2 * (m - (ITEM_B + 2)) + k // 4
                    if k % 4 == 0 and 0 <= hb < B_HEADS:
                        b_softplus(hb)
                    if k % 4 == 1 and 1 <= hb <= B_HEADS:
                        b_weights(hb - 1)
                    if (m, k) in UNIT_AT:
                        c_unit(UNIT_AT[(m, k)])
                    if (m, k) == (ITEM_COMBINE - 1, 0):
                        to_token_order()
                    if (m, k) == (ITEM_COMBINE, 2):
                        act.wait_ge(cmb, 5)
                        act.activation(CW[:, 1:4, :], CW[:, 1:4, :], ACT.Exp).then_inc(cmb_e, 1)
                    if m >= ITEM_TURN and k % 4 == 2 and 2 * (m - ITEM_TURN) + k // 4 < KT:
                        ft = 2 * (m - ITEM_TURN) + k // 4
                        act.wait_ge(yt_done, ft + 1)
                        act.activation(YH[ft][:, :], PS[:, 2 + ft % 4, :], ACT.Copy).then_inc(yt_high, 1)

                def gate_sigmoids(i0, i1):
                    for i in range(i0, i1):
                        act.wait_ge(*taken(TILE0[ITEM_GATE] + i))
                        act.activation(GT[i][:, :], GT[i][:, :], ACT.Sigmoid).then_inc(g_sig, 1)

                def next_high_part(u):
                    act.wait_ge(next_loaded[u], 32)
                    act.wait_ge(*used(NG - 2 + u))
                    act.activation(WH[u][:, :], RAW[u][:, :], ACT.Copy).then_inc(next_high, 1)

                pre(0)
                inputs(0)
                ffn_in(0, G_FFN1)
                row_groups(G_FO1, FO - 1)
                post(0)
                high(G_MIX + 1)
                pre(1)
                inputs(1)
                for m in range(NM):
                    for k in range(8):
                        if 1 <= k <= 4 and m:
                            if m + 1 < NM:
                                high_part(m + 1, k - 1)
                            elif k == 1:
                                high(G_BR)
                        mixers(m, k)
                        if m >= ITEM_TURN and k == 7:
                            gate_sigmoids(3 * (m - ITEM_TURN), min(3 * (m - ITEM_TURN) + 3, 23))
                gate_sigmoids(23, 24)
                high(G_BR + 1)
                for q in range(4):
                    for u in range(2):
                        j = 2 * q + u
                        act.wait_ge(br_sum, j + 1)
                        act.activation(HH[:, j, :], MA[j % 2][:, 0, :], ACT.Copy).then_inc(m_high, 1)
                    high(G_BR + q + 2)
                row_groups(G_WO, 3)
                post(1)
                high(G_WO + 5)
                pre(2)
                inputs(2)
                ffn_in(1, G_FFN2)
                row_groups(G_FO2, FO - 1)
                next_high_part(0)
                post(2)

            @block.vector
            def _(dve):
                dve.tensor_scalar(OML[:, :], LB[:, bass.ds(l, 1), :].rearrange("p o h -> p (o h)"),
                                  -1.0, 1.0, ALU.mult, ALU.add).then_inc(lb_out, 1)

                dve.tensor_copy(LBC[:, :], LB[:, bass.ds(l, 1), :].rearrange("p o h -> p (o h)")).then_inc(ada_part, KT)

                def columns(c0, c1, before, pre_of, post_of):
                    dve.tensor_tensor(MOD[:, c0:c1], MOD[:, c0:c1],
                                      COLS[:, bass.ds(l, 1), c0:c1].rearrange("p o c -> p (o c)"), ALU.add).then_inc(
                                          ada_cols, 1)
                    dve.wait_ge(ada_cols, before + 1)
                    mod = MOD[:, :].rearrange("p (s v k) -> p s v k", s=3, v=3)
                    gains = COLS[:, bass.ds(l, 1), 72:120].rearrange("p o (s u k) -> p (o s) u k", s=3, u=2)
                    for s in pre_of:
                        dve.scalar_tensor_tensor(PRE[:, s, :], mod[:, s, 1, :], 1.0, gains[:, s, 0, :],
                                                 ALU.add, ALU.mult).then_inc(ada_cols, 1)
                    for s in post_of:
                        dve.scalar_tensor_tensor(POST[:, s, :], mod[:, s, 2, :], 1.0 if s == 1 else 0.5,
                                                 gains[:, s, 1, :], ALU.mult, ALU.mult).then_inc(ada_cols, 1)

                columns(0, 4 * ADA_FIRST, 0, (0,), ())
                dve.wait_ge(ada_cols, 2)

                def add_halves(n, q):
                    dve.wait_ge(n_sq, KT * n + 2 * q + 2)
                    dve.wait_ge(n_mm, 4 * n)
                    dve.tensor_tensor(NSS[q][:, :], NSQ[q % 2][:, 0, :], NSQ[q % 2][:, 1, :], ALU.add).then_inc(n_ss, 1)

                def post(s):
                    for j in range(KT):
                        dve.wait_ge(n_sq, KT * (2 * s + 1) + j + 1)
                        if j % 2:
                            add_halves(2 * s + 1, j // 2)
                        dve.tensor_scalar(Y[:, j, :], PS[:, j, :], POST[:, s, j:j + 1], None, ALU.mult).then_inc(
                            y_copied, 1)
                    dve.wait_ge(n_r, 2 * s + 2)
                    for j in range(KT):
                        dve.tensor_tensor(Y[:, j, :], Y[:, j, :], NR[:, :], ALU.mult).then_inc(y_scaled, 1)
                        if j % 2:
                            dve.wait_ge(y_scaled, KT * s + j + 1)
                            dve.tensor_tensor(X[:, j, :], X[:, j, :], Y[:, j, :], ALU.add).then_inc(x_odd, 1)
                            if j > 1 and s < 2:
                                add_halves(2 * s + 2, j // 2 - 1)

                def low_of_input(s, j):
                    dve.wait_ge(h_high, KT * s + j + 1)
                    dve.scalar_tensor_tensor(HL[:, j, :], U[:, j, :], MOD[:, 24 * s + j:24 * s + j + 1],
                                             HH[:, j, :].bitcast(F32), ALU.add, ALU.subtract).then_inc(h_low_even, 1)

                def pre(s):
                    for q in range(3 if s else 0, 4):
                        add_halves(2 * s, q)
                    dve.wait_ge(n_r, 2 * s + 1)
                    for j in range(KT):
                        dve.scalar_tensor_tensor(U[:, j, :], X[:, j, :], PRE[:, s, j:j + 1], NR[:, :],
                                                 ALU.mult, ALU.mult).then_inc(u_done, 1)
                        if j in (1, 3, 5, 7):
                            low_of_input(s, j - 1)

                def ffn_in(f, g0):
                    ffn_pair(f, g0, 0, (range(KT), ()), 0)
                    n = ADA_CHUNKS[f]
                    for first, end in ((1, n),) if f == 0 else ((1, ADA_OWN), (ADA_OWN, n), (n, FI // 2)):
                        with dve.Fori(first, end) as i:
                            ffn_pair(f, g0, i, (range(4), range(4, KT)) if end <= n else None, first)

                def ffn_pair(f, g0, i, ada, first):
                    for u in range(2):
                        if ada:
                            for k in ada[u]:
                                acc, w = AACC[0][:, :], AW[k % 2][:, :]
                                dve.wait_ge(ada_in[k % 2], i * (16 * KT // 2) + 16 * (ADA_BEFORE[f] * KT // 2 + k // 2 + 1))
                                if k == 0:
                                    ins = dve.tensor_scalar(acc, w, CC[:, k:k + 1], None, ALU.mult)
                                else:
                                    dve.wait_ge(ada_part, i * KT + ((ADA_BEFORE[f] + 1) * KT + k))
                                    ins = dve.scalar_tensor_tensor(acc, w, CC[:, k:k + 1], acc, ALU.mult, ALU.add)
                                ins.then_inc(ada_part, 1)
                        n = FT * f + u + 1
                        dve.wait_ge(silu_done, i * 2 + n)
                        dve.wait_ge(w_used, i * 2 + used_count(g0 + u))
                        dve.tensor_tensor(SB[u][:, :], SB[u][:, :], PS[:, 2 * u + 1, :], ALU.mult).then_inc(gated, 1)
                        dve.wait_ge(g_high, i * 2 + n)
                        gh = GH[:, bass.ds(i * 2 + u, 1), :].rearrange("p o c -> p (o c)")
                        gl = GL[:, bass.ds(i * 2 + u, 1), :].rearrange("p o c -> p (o c)")
                        dve.tensor_tensor(gl, SB[u][:, :], gh.bitcast(F32), ALU.subtract).then_inc(g_low, 1)
                    if ada:
                        dve.wait_ge(ada_sum, i + (ADA_BEFORE[f] + 1))
                        ch0 = ADA_FIRST if f == 0 else ADA_ALL - ADA_OWN if first < ADA_OWN else -ADA_OWN
                        dve.tensor_copy(MOD[:, bass.ds(i * 4 + 4 * ch0, 4)], PS[:, 4, 0:4]).then_inc(ada_out, 1)

                def take(m, i):
                    kind, c0, width = MIX[m]
                    if kind == "a":
                        return
                    dve.wait_ge(*projected(m, i))
                    tile = TILE0[m] + i
                    ps = PS[:, tile % 2, :]
                    if kind == "av":
                        c = c0 - COL_AI
                        ins = dve.tensor_copy(AV[:, i, c:c + width], ps[:, 0:width])
                    elif kind == "ag":
                        c = c0 - COL_AG
                        ins = dve.tensor_copy(GN[:, i, c:c + width], ps[:, 0:width])
                    elif kind == "bv":
                        c = c0 - COL_BV
                        ins = dve.tensor_copy(BV[:, i, c:c + width], ps[:, 0:width])
                    elif kind == "b":
                        p = m - ITEM_B
                        dve.wait_ge(b_z, 2 * max(p - 1, 0))
                        ins = dve.tensor_scalar(BQ[p % 2][:, :], ps, QSCALE, None, ALU.mult) if i == 0 else \
                            dve.tensor_copy(BK[p % 2][:, :], ps)
                    elif kind == "cv":
                        gi = (c0 - COL_CV) // 256
                        ins = dve.tensor_copy(CV[:, i, 4 * gi:4 * gi + 4, 0:HD], ps[:, 0:256].rearrange("p (h d) -> p h d", d=HD))
                    elif kind == "c":
                        p = m - ITEM_C
                        if p >= 2:
                            dve.wait_ge(c_s, units_of(p - 2)[-1] + 1)
                        dst = (CQ, CK)[i][p % 2][:, :]
                        if p >= 2:
                            dst, ps = dst.rearrange("p (c i) -> p c i", c=4), ps.rearrange("p (i c) -> p c i", c=4)
                        ins = dve.tensor_scalar(dst, ps, QSCALE, None, ALU.mult) if i == 0 else dve.tensor_copy(dst, ps)
                    else:
                        ins = dve.tensor_copy(GT[2 * (m - ITEM_GATE) + i][:, :], ps)
                    ins.then_inc(tile_out[tile % 2], 1)

                def a_prepare(h, k):
                    if k == 0:
                        dve.wait_ge(*taken(TILE0[2 * h] + 1))
                    if k == 1:
                        dve.wait_ge(p_ln, h + 1)
                        dve.scalar_tensor_tensor(W2[:, :, :], QF[:, :, :], 0.0, W1[:, :, :], ALU.min, ALU.subtract).then_inc(
                            p_ls, 1)
                        dve.wait_ge(p_ls, h + 1)
                        dve.wait_ge(i_diag, max(h - 1, 0))
                        dve.tensor_tensor(AK[h % 2][:, :], W2[:, 1, :], QF[:, 1, :], ALU.subtract).then_inc(p_t, 1)
                    if k == 3:
                        dve.wait_ge(p_sg, h + 1)
                        dve.tensor_tensor(AQ[h % 2][:, :], QF[:, 0, :], W2[:, 0, :], ALU.mult).then_inc(p_q, 1)
                        dve.tensor_scalar(W1[:, 0, :], W2[:, 1, :], OML[:, h:h + 1], LBC[:, h:h + 1], ALU.mult, ALU.add).then_inc(
                            p_f, 1)
                        dve.wait_ge(p_f, 3 * h + 1)
                        dve.tensor_scalar(W1[:, 1, :], W1[:, 0, :], TINY, 1.0 / LN_LIFT * 2, ALU.max, ALU.min).then_inc(
                            p_f, 1)
                        dve.wait_ge(p_log, 3 * h)
                        dve.tensor_scalar(MK[:, :], W1[:, 0, :], 1.0 / LN_LIFT, None, ALU.is_lt).then_inc(p_mask, 1)
                        dve.wait_ge(p_mask, h + 1)
                        dve.tensor_scalar(W1[:, 0, :], W1[:, 0, :], 1.0 / LN_LIFT, None, ALU.max).then_inc(p_f, 1)
                    if k == 6:
                        dve.wait_ge(p_lf, 2 * h + 2)
                        dve.tensor_scalar(W1[:, 1, :], W1[:, 1, :], -math.log(LN_LIFT), None, ALU.add).then_inc(p_log, 1)
                        dve.wait_ge(p_log, 3 * h + 1)
                        dve.wait_ge(p_mask, h + 1)
                        dve.copy_predicated(AB[h % 2][:, :], MK[:, :], W1[:, 1, :]).then_inc(p_log, 1)
                        dve.wait_ge(p_log, 3 * h + 2)
                        dve.tensor_tensor_scan(AB[h % 2][:, :], const("reset"), AB[h % 2][:, :], 0.0, ALU.mult, ALU.add).then_inc(
                            p_log, 1)

                def level_out(h, k):
                    n = A_LEVELS * h + k
                    dve.wait_ge(v_mm, n + 1)
                    dve.wait_ge(v_out, n)
                    half, keys = P >> (k + 1), level_keys(k)
                    dve.copy_predicated(
              AS[h % 2][0:keys, :, :].rearrange("p c (b w) -> p c b w", w=2 * half)[:, :, :, half:],
              LM[0:keys, k, :].rearrange("p (b r) -> p b r", r=half).unsqueeze(1).broadcast_to(
                  [keys, TT, 64 // half, half]),
              PS[0:keys, 2 + n % 2, 0:256].rearrange("p (c b r) -> p c b r", c=TT, r=half)).then_inc(v_out, 1)

                def a_head(h, k):
                    aq, ab, ak, s = AQ[h % 2], AB[h % 2], AK[h % 2], AS[h % 2]
                    if k < A_LEVELS:
                        n = A_LEVELS * h + k
                        dve.wait_ge(v_decay, n + 1)
                        dve.wait_ge(v_mm, max(n - 1, 0))
                        if n == 0:
                            dve.wait_ge(kl_set, 2)
                        dve.wait_ge(p_k, h + 1)
                        dve.wait_ge(p_q, h + 1)
                        dve.tensor_tensor(level_view(KL[n % 2][:, :], k, 0), level_view(ak[:, :], k, 0),
                                          level_view(AE[n % 2][:, :], k, 0), ALU.mult)
                        dve.tensor_tensor(
               QL[n % 2][:, :, :].rearrange("p c t -> p (c t)").rearrange("p (b r) -> p b r", r=P >> (k + 1)),
               level_view(aq[:, :], k, 1), level_view(AE[n % 2][:, :], k, 1), ALU.mult).then_inc(v_scaled, 1)
                    if k == 0:
                        dve.wait_ge(p_log, 3 * h + 3)
                        dve.wait_ge(i_turn, h)
                        b = level_view(ab[:, :], 0)
                        dve.tensor_tensor(level_view(KD[:, :], 0), b, b[:, :, P - 1:P].broadcast_to([P, TT, P]),
                                          ALU.subtract).then_inc(i_diff, 1)
                        dve.wait_ge(i_diag, h + 1)
                        dve.wait_ge(i_o, max(h - 1, 0))
                        dve.tensor_tensor(s[:, :, :], PS[:, 4, :].rearrange("p (c t) -> p c t", c=TT),
                                          ident.unsqueeze(1).broadcast_to([P, TT, P]), ALU.mult).then_inc(i_s0, 1)
                        dve.wait_ge(i_s0, h + 1)
                    if k == 1:
                        dve.wait_ge(i_eb, h + 1)
                        dve.tensor_tensor(QB[h % 2][:, :], aq[:, :], EB[:, :], ALU.mult).then_inc(i_qb, 1)
                        dve.wait_ge(i_decay, h + 1)
                        dve.tensor_tensor(KD[:, :], KD[:, :], ak[:, :], ALU.mult).then_inc(i_kd, 1)
                    if k == 6:
                        dve.wait_ge(i_u, h + 1)
                        st = ST[h % 2]
                        dve.tensor_copy(st[:, 0, :], PS[:, 6, 0:A_V]).then_inc(i_st, 1)
                        for c in (1, 2):
                            dve.wait_ge(i_st, 3 * h + c)
                            dve.scalar_tensor_tensor(st[:, c, :], st[:, c - 1, :], EB[:, (c + 1) * P - 1:(c + 1) * P],
                                                     PS[:, 6, c * A_V:(c + 1) * A_V], ALU.mult, ALU.add).then_inc(i_st, 1)
                    if 2 <= k:
                        level_out(h, k - 2)

                def a_output(h):
                    dve.wait_ge(i_o, h + 1)
                    dve.tensor_copy(OA[:, :, h * A_V:(h + 1) * A_V],
                                    PS[:, 7, 0:256].rearrange("p (c d) -> p c d", c=TT)).then_inc(i_oout, 1)

                def a_norm(k):
                    sq = ASQ[:, :, :].rearrange("p t (h d) -> p (t h) d", d=A_V)
                    oa = OA[:, :, :].rearrange("p t (h d) -> p (t h) d", d=A_V)
                    gn = GN[:, :, :].rearrange("p t (h d) -> p (t h) d", d=A_V)
                    if k == 4:
                        dve.wait_ge(i_oout, A_HEADS)
                        dve.tensor_tensor(sq, oa, oa, ALU.mult).then_inc(an, 1)
                        dve.wait_ge(an, 1)
                        dve.tensor_reduce(ARS[:, 0, :], sq, AX.X, ALU.add).then_inc(an, 1)
                        dve.wait_ge(gn_silu, 1)
                        dve.tensor_tensor(gn, gn, NGR[:, :].unsqueeze(1).broadcast_to([P, TT * A_HEADS, A_V]), ALU.mult).then_inc(
                            an, 1)
                    if k == 6:
                        dve.wait_ge(an_r, 1)
                        dve.tensor_tensor(oa, oa, ARS[:, 2, :].unsqueeze(2).broadcast_to([P, TT * A_HEADS, A_V]), ALU.mult).then_inc(
                            an, 1)
                        dve.wait_ge(an, 4)
                        dve.tensor_tensor(oa, oa, gn, ALU.mult).then_inc(an, 1)

                def b_softplus(h):
                    dve.wait_ge(b_ln, h + 1)
                    dve.wait_ge(b_arg, max(h - 1, 0))
                    s, z, o = 3 * (h % 2), BZ[h % 2], BS[h % 2]
                    dve.scalar_tensor_tensor(o[:, 0:512], PS[:, 2 + s, :], 0.0, z[:, 0:512], ALU.max, ALU.add)
                    dve.scalar_tensor_tensor(o[:, 512:1024], PS[:, 3 + s, :], 0.0, z[:, 512:1024], ALU.max, ALU.add)
                    dve.scalar_tensor_tensor(o[:, 1024:1280], PS[:, 4 + s, 0:256], 0.0, z[:, 1024:1280], ALU.max, ALU.add).then_inc(
                        b_sp, 1)

                def b_output(h):
                    dve.wait_ge(b_pv, h + 1)
                    dve.tensor_copy(OB[:, :, h * HD:(h + 1) * HD],
                                    PS[:, 4 + 3 * (h % 2), 256:512].rearrange("p (c d) -> p c d", c=TT)).then_inc(
                                        b_out, 1)

                def c_unit(n):
                    if n < NU:
                        h, t0 = units[n]
                        wide = h < C_SLOTS
                        nt, keys = (2, 2 * P) if wide else (4, P)
                        dve.wait_ge(c_s, n + 1)
                        dve.wait_ge(c_p, max(n - 1, 0))
                        cs = CS[n % 2][:, :].rearrange("p (t s) -> p t s", t=nt)
                        if wide:
                            dist = const("del0")[:, t0 * 2 * P:(t0 + 2) * 2 * P].rearrange("p (t s) -> p t s", t=nt)
                        else:
                            dist = const("del1" if h < 8 else "del2").unsqueeze(1).broadcast_to([P, 4, P])
                        dve.scalar_tensor_tensor(cs, dist, slopes[h], PS[:, 2 + n % 2, :].rearrange("p (t s) -> p t s", t=nt),
                                                 ALU.mult, ALU.add).then_inc(c_bias, 1)
                        dve.wait_ge(c_bias, n + 1)
                        most = OC[:, t0:t0 + nt, h, HD + 1:HD + 2]
                        dve.tensor_reduce(most, cs, AX.X, ALU.max).then_inc(c_max, 1)
                        dve.wait_ge(c_max, n + 1)
                        dve.tensor_tensor(cs, cs, most.broadcast_to([P, nt, keys]), ALU.subtract).then_inc(c_sub, 1)
                    if n >= 2:
                        q = n - 2
                        h, t0 = units[q]
                        nt = 2 if h < C_SLOTS else 4
                        dve.wait_ge(c_pv, q + 1)
                        dve.tensor_copy(OC[:, t0:t0 + nt, h, 0:HD + 1],
                                        PS[:, 6 + q % 2, 0:nt * 65].rearrange("p (t d) -> p t d", t=nt)).then_inc(
                                            c_out, 1)

                def combine(k):
                    o = [OC[:, :, 0:4, :], OCN[:, :, 0:4, :], OCN[:, :, 4:8, :]]
                    mx = [x[:, :, :, HD + 1] for x in o]
                    w = [CW[:, i, :].rearrange("p (t h) -> p t h", t=TT) for i in range(5)]
                    if k == 0:
                        dve.wait_ge(c_perm, 256)
                        dve.tensor_tensor(w[0], mx[0], mx[1], ALU.max).then_inc(cmb, 1)
                        dve.wait_ge(cmb, 1)
                        dve.tensor_tensor(w[0], w[0], mx[2], ALU.max).then_inc(cmb, 1)
                        dve.wait_ge(cmb, 2)
                        for g in range(3):
                            dve.tensor_tensor(w[1 + g], mx[g], w[0], ALU.subtract).then_inc(cmb, 1)
                    if k == 3:
                        dve.wait_ge(cmb_e, 1)

                        def part(dst, g):
                            return dve.tensor_tensor(dst[:, :, :, :], o[g][:, :, :, 0:HD + 1],
                                                     w[1 + g].unsqueeze(3).broadcast_to([P, TT, C_SLOTS, HD + 1]), ALU.mult)

                        part(CX[0], 0)
                        part(CX[1], 1).then_inc(cmb, 1)
                        dve.wait_ge(cmb, 6)
                        dve.tensor_tensor(CX[0][:, :, :, :], CX[0][:, :, :, :], CX[1][:, :, :, :], ALU.add).then_inc(
                            cmb, 1)
                        dve.wait_ge(cmb, 7)
                        part(CX[1], 2).then_inc(cmb_x, 1)
                        dve.wait_ge(cmb_x, 1)
                        dve.tensor_tensor(CX[0][:, :, :, :], CX[0][:, :, :, :], CX[1][:, :, :, :], ALU.add).then_inc(
                            cmb, 1)
                        dve.wait_ge(cmb, 8)
                        dve.reciprocal(w[4], CX[0][:, :, :, HD]).then_inc(cmb, 1)
                        dve.wait_ge(cmb, 9)
                        dve.tensor_tensor(OF[:, :, :].rearrange("p t (h d) -> p t h d", d=HD), CX[0][:, :, :, 0:HD],
                                          w[4].unsqueeze(3).broadcast_to([P, TT, C_SLOTS, HD]), ALU.mult).then_inc(cmb, 1)

                def mixers(m, k):
                    if k == 0 and m:
                        take(m - 1, TILE0[m] - TILE0[m - 1] - 1)
                    if m % 2 and m < 2 * A_HEADS:
                        a_prepare(m // 2, k)
                    if MIX[m][0] in TOKEN_KINDS:
                        if k in (2, 4, 6):
                            take(m, k // 2 - 1)
                    elif k == 4:
                        take(m, 0)
                    if m % 2 == 0 and 0 < m <= 2 * A_HEADS:
                        a_head(m // 2 - 1, k)
                    if m % 2 and 3 <= m <= 2 * A_HEADS + 1:
                        if k == 0:
                            level_out((m - 3) // 2, A_LEVELS - 1)
                        if k == 3:
                            a_output((m - 3) // 2)
                    if m == ITEM_B + 1:
                        a_norm(k)
                    hb = 2 * (m - (ITEM_B + 2)) + k // 4
                    if k % 4 == 2 and 0 <= hb < B_HEADS:
                        b_softplus(hb)
                    if k % 4 == 3 and 1 <= hb <= B_HEADS:
                        b_output(hb - 1)
                    if (m, k) in UNIT_AT:
                        c_unit(UNIT_AT[(m, k)])
                    if m == ITEM_COMBINE:
                        combine(k)
                    if m >= ITEM_TURN and k % 4 == 2 and 2 * (m - ITEM_TURN) + k // 4 < KT:
                        ft = 2 * (m - ITEM_TURN) + k // 4
                        dve.wait_ge(yt_high, ft + 1)
                        dve.tensor_tensor(YL[ft][:, :], PS[:, 2 + ft % 4, :], YH[ft][:, :].bitcast(F32), ALU.subtract).then_inc(
                            yt_low, 1)

                pre(0)
                ffn_in(0, G_FFN1)
                dve.wait_ge(ada_out, ADA_CHUNKS[0])
                columns(4 * ADA_FIRST, 4 * (ADA_ALL - ADA_OWN), 2, (1, 2), (0, 1))
                dve.wait_ge(ada_cols, 7)
                post(0)
                pre(1)
                for m in range(NM):
                    for k in range(8):
                        mixers(m, k)
                take(NM - 1, 1)
                for j in range(KT):
                    if j % 2:
                        dve.wait_ge(*used(G_BR + j // 2))
                    else:
                        dve.wait_ge(br_done, j // 2 + 1)
                    dve.wait_ge(g_sig, 24)
                    dve.wait_ge(m_low, max(j - 1, 0))
                    for n in range(3):
                        ins = dve.tensor_tensor(MA[j % 2][:, n, :], PS[:, 3 * (j % 2) + n, :], GT[8 * n + j][:, :], ALU.mult)
                    ins.then_inc(br_mul, 1)
                    dve.wait_ge(br_mul, j + 1)
                    dve.tensor_tensor(MA[j % 2][:, 0, :], MA[j % 2][:, 0, :], MA[j % 2][:, 1, :], ALU.add).then_inc(
                        br_add, 1)
                post(1)
                pre(2)
                ffn_in(1, G_FFN2)
                dve.wait_ge(ada_out, ADA_ALL)
                columns(4 * (ADA_ALL - ADA_OWN), 72, 7, (), (2,))
                dve.wait_ge(ada_cols, 9)
                post(2)

            @block.gpsimd
            def _(pool):
                def low(g):
                    slot, n = g % 2, group_columns(g)
                    pool.wait_ge(w_high, g + 1)
                    pool.tensor_tensor(WL[slot][:, 0:n], RAW[slot][:, 0:n], WH[slot][:, 0:n].bitcast(F32),
                                       ALU.subtract).then_inc(w_low, 1)

                def low_part(m, q):
                    g = G_MIX + m
                    slot, n = g % 2, group_columns(g) // 4
                    part = slice(q * n, (q + 1) * n)
                    if q == 3:
                        pool.wait_ge(w_high, g + 1)
                    else:
                        pool.wait_ge(part_high, 3 * (m - 2) + q + 1)
                    ins = pool.tensor_tensor(WL[slot][:, part], RAW[slot][:, part], WH[slot][:, part].bitcast(F32), ALU.subtract)
                    if q == 3:
                        ins.then_inc(w_low, 1)

                def post(s):
                    for j in range(0, KT, 2):
                        pool.wait_ge(y_scaled, KT * s + j + 1)
                        pool.tensor_tensor(X[:, j, :], X[:, j, :], Y[:, j, :], ALU.add).then_inc(x_even, 1)

                def pre(s):
                    for j in range(1, KT, 2):
                        pool.wait_ge(h_high, KT * s + j + 1)
                        pool.tensor_scalar(U[:, j, :], U[:, j, :], 1.0, MOD[:, 24 * s + j:24 * s + j + 1],
                                           ALU.mult, ALU.add).then_inc(f_odd, 1)
                        pool.wait_ge(f_odd, 4 * s + j // 2 + 1)
                        pool.tensor_tensor(HL[:, j, :], U[:, j, :], HH[:, j, :].bitcast(F32), ALU.subtract).then_inc(
                            h_low_odd, 1)

                def ffn_in(g0):
                    with pool.Fori(0, FI // 2) as i:
                        for u in range(2):
                            slot = (g0 + u) % 2
                            pool.wait_ge(w_high, i * 2 + (g0 + u + 3))
                            pool.tensor_tensor(WL[slot][:, :], RAW[slot][:, :], WH[slot][:, :].bitcast(F32),
                                               ALU.subtract).then_inc(w_low, 1)

                def row_groups(g0, n):
                    for i in range(n):
                        if g0 + i + 2 < NG:
                            low(g0 + i + 2)

                def a_diff(h, k):
                    n = A_LEVELS * h + k
                    pool.wait_ge(p_log, 3 * h + 3)
                    pool.wait_ge(v_decay, max(n - 1, 0))
                    w = P >> k
                    b = level_view(AB[h % 2][:, :], k)
                    pool.tensor_tensor(level_view(AD[n % 2][:, :], k), b,
                                       b[:, :, w // 2 - 1:w // 2].broadcast_to([P, SEQ // w, w]), ALU.subtract).then_inc(
                                           v_diff, 1)

                def a_head(h, k):
                    if k == 0:
                        pool.wait_ge(p_k, h + 1)
                        pool.wait_ge(p_q, h + 1)
                        pool.wait_ge(i_o, max(h - 1, 0))
                        pool.tensor_tensor(QB[h % 2][:, :], AQ[h % 2][:, :], AK[h % 2][:, :], ALU.mult).then_inc(i_qk, 1)
                    if k < A_LEVELS:
                        a_diff(h, k)

                def mixers(m, k):
                    if m % 2 == 0 and 0 < m <= 2 * A_HEADS:
                        a_head(m // 2 - 1, k)
                    if (m, k) == (1, 0):
                        for i in range(2):
                            pool.memset(KL[i][:, :], 0.0).then_inc(kl_set, 1)
                    hb = 2 * (m - (ITEM_B + 2)) + k // 4
                    if k % 4 == 2 and 0 <= hb < B_HEADS:
                        pool.wait_ge(b_sp, hb + 1)
                        for i in range(TT):
                            a = BS[hb % 2][:, ZCOL[i]:ZCOL[i] + P]
                            ins = pool.tensor_tensor(a, a, const("strict"), ALU.mult)
                        ins.then_inc(b_spm, 1)
                    if (m, k) == (ITEM_B + 3, 0):
                        pool.wait_ge(i_oout, A_HEADS)
                        pool.memset(CV[:, :, :, HD:HD + 1], 1.0).then_inc(c_ones, 1)

                def next_low_part(u):
                    pool.wait_ge(next_high, u + 1)
                    pool.tensor_tensor(WL[u][:, :], RAW[u][:, :], WH[u][:, :].bitcast(F32), ALU.subtract)

                pre(0)
                ffn_in(G_FFN1)
                row_groups(G_FO1, FO - 1)
                post(0)
                low(G_MIX + 1)
                pre(1)
                for m in range(NM):
                    for k in range(8):
                        mixers(m, k)
                        if 1 <= k <= 4 and m:
                            if m + 1 < NM:
                                low_part(m + 1, k - 1)
                            elif k == 1:
                                low(G_BR)
                low(G_BR + 1)
                for q in range(4):
                    for u in range(2):
                        j = 2 * q + u
                        ma = MA[j % 2]
                        pool.wait_ge(br_add, j + 1)
                        pool.tensor_tensor(ma[:, 0, :], ma[:, 0, :], ma[:, 2, :], ALU.add).then_inc(br_sum, 1)
                        pool.wait_ge(br_sum, j + 1)
                        pool.wait_ge(m_high, j + 1)
                        pool.tensor_tensor(HL[:, j, :], ma[:, 0, :], HH[:, j, :].bitcast(F32), ALU.subtract).then_inc(
                            m_low, 1)
                    low(G_BR + q + 2)
                row_groups(G_WO, 3)
                post(1)
                low(G_WO + 5)
                pre(2)
                ffn_in(G_FFN2)
                row_groups(G_FO2, FO - 1)
                next_low_part(0)
                next_low_part(1)
                post(2)

        with nc.Block() as block:
            @block.gpsimd
            def _(pool):
                pool.sem_clear(range(semaphores[0].num, semaphores[-1].num + 1))
                count_first_groups(pool)

    with nc.Block() as block:
        @block.sync
        def _(sp):
            for i in range(TT):
                sp.wait_ge(res_out, 2 * (i + 1))
                sp.dma_start(out[0, i * P:(i + 1) * P, :], XIN[:, i, :]).then_inc(stored, 16)
            sp.wait_ge(stored, 16 * TT)

        @block.tensor
        def _(pe):
            for i in range(TT):
                for half in range(2):
                    n = 2 * i + half
                    if n >= 2:
                        pe.wait_ge(res_out, n - 1)
                    for k in range(4):
                        mm = pe.transpose(PS[:, 1 + n % 2, k * P:(k + 1) * P], X[:, 4 * half + k, i * P:(i + 1) * P], ident)
                    mm.then_inc(res_turned, 1)

        @block.vector
        def _(dve):
            for n in range(2 * TT):
                dve.wait_ge(res_turned, n + 1)
                dve.tensor_copy(XIN[:, n // 2, (n % 2) * 512:(n % 2) * 512 + 512], PS[:, 1 + n % 2, :]).then_inc(
                    res_out, 1)


_INS = ["x", "c", "w_ada", "b_ada", "norm_g", "ffn1_w_in", "ffn1_w_out", "w_in", "hgrn_lb_logits", "hgrn_norm_g",
        "w_branch_a", "w_branch_b", "w_branch_c", "w_out", "ffn2_w_in", "ffn2_w_out"]


def kernel(**inputs):
    import concourse.bacc as bacc
    from concourse.bass_utils import run_bass_kernel_spmd

    nc = bacc.Bacc("TRN2", target_bir_lowering=False, num_devices=1)
    arrays = {name: np.ascontiguousarray(inputs[name]) for name in _INS}
    arrays["const_f"], arrays["const_m"] = constants(), level_masks()
    t = {name: nc.dram_tensor(f"in_{name}", a.shape, mybir.dt.from_np(a.dtype), kind="ExternalInput").ap()
         for name, a in arrays.items()}
    out = nc.dram_tensor("out", (1, SEQ, D), F32, kind="ExternalOutput").ap()
    build(nc, t, out)
    r = run_bass_kernel_spmd(nc, [{f"in_{name}": a for name, a in arrays.items()}], core_ids=[0])
    return r.results[0]["out"]
```
